# Optimizing a Trainium2 kernel written in Bass

```python
import math
import jax
import jax.numpy as jnp
from jax import lax
import numpy as np

D_MODEL = 2048
BATCH = 1
SEQ = 256
DEPTH = 1

S5_GROUP_CH = 16
S5_STATE = 64
S5_WIDTH = D_MODEL
S5_GROUPS = S5_WIDTH // S5_GROUP_CH
DT_MIN = 1e-3
DT_MAX = 1e-1
DN_QK_HEADS = 16
DN_V_HEADS = 32
DN_HEAD_DIM = 128
DN_KEY_WIDTH = DN_QK_HEADS * DN_HEAD_DIM
DN_VALUE_WIDTH = DN_V_HEADS * DN_HEAD_DIM
DN_CONV_CH = 2 * DN_KEY_WIDTH + DN_VALUE_WIDTH
DN_CONV = 4
DN_CHUNK = 64
N_EXPERTS = 32
TOP_K = 4
D_EXPERT = 512
SWIGLU_LIMIT = 7.0
SWIGLU_ALPHA = 1.702
MOE_BLOCK = 128
DEEPNORM_ALPHA = (2 * DEPTH) ** 0.25
DEEPNORM_BETA = (8 * DEPTH) ** -0.25
LN_EPS = 1e-5
RMS_EPS = 1e-6
L2_EPS = 1e-6
S5_MAX_REAL = -1e-4
OFF_S5 = 0
OFF_QKV = OFF_S5 + S5_WIDTH
OFF_Z = OFF_QKV + DN_CONV_CH
OFF_BETA = OFF_Z + DN_VALUE_WIDTH
OFF_DECAY = OFF_BETA + DN_V_HEADS
OFF_GATE_S5 = OFF_DECAY + DN_V_HEADS
OFF_GATE_DN = OFF_GATE_S5 + D_MODEL
IN_COLS = OFF_GATE_DN + D_MODEL

kernel_name = 'hybrid_s5_gdn_moe_deepnorm'

def layer_norm(x, g, b):
    xf = x.astype(jnp.float32)
    mu = jnp.mean(xf, axis=-1, keepdims=True)
    var = jnp.mean(jnp.square(xf - mu), axis=-1, keepdims=True)
    y = (xf - mu) * lax.rsqrt(var + LN_EPS) * g.astype(jnp.float32) + b.astype(jnp.float32)
    return y.astype(x.dtype)

def l2_normalize(t):
    return t * lax.rsqrt(jnp.sum(jnp.square(t), axis=-1, keepdims=True) + L2_EPS)

def causal_depthwise_conv(x, w):
    T = x.shape[1]
    K = w.shape[1]
    xp = jnp.pad(x, ((0, 0), (K - 1, 0), (0, 0)))
    out = xp[:, 0:T, :] * w[:, 0]
    for j in range(1, K):
        out = out + xp[:, j:j + T, :] * w[:, j]
    return out

def s5_branch(u, lam_re, lam_im, log_dt, b_re, b_im, c_re, c_im, d_skip, w_glu_a, w_glu_b):
    f32 = jnp.float32
    bsz, T, _ = u.shape
    u = u.astype(f32).reshape(bsz, T, S5_GROUPS, S5_GROUP_CH)
    lre = jnp.minimum(lam_re.astype(f32), S5_MAX_REAL)
    lim = lam_im.astype(f32)
    dt = jnp.exp(log_dt.astype(f32))[:, None]
    mag = jnp.exp(lre * dt)
    a_re = mag * jnp.cos(lim * dt)
    a_im = mag * jnp.sin(lim * dt)
    den = jnp.square(lre) + jnp.square(lim)
    f_re = ((a_re - 1.0) * lre + a_im * lim) / den
    f_im = (a_im * lre - (a_re - 1.0) * lim) / den
    br = b_re.astype(f32)
    bi = b_im.astype(f32)
    bb_re = f_re[..., None] * br - f_im[..., None] * bi
    bb_im = f_re[..., None] * bi + f_im[..., None] * br
    bu_re = jnp.einsum('btgp,gnp->btgn', u, bb_re)
    bu_im = jnp.einsum('btgp,gnp->btgn', u, bb_im)
    lam_bar_re = jnp.broadcast_to(a_re, bu_re.shape)
    lam_bar_im = jnp.broadcast_to(a_im, bu_im.shape)

    def combine(earlier, later):
        ar1, ai1, br1, bi1 = earlier
        ar2, ai2, br2, bi2 = later
        return (ar2 * ar1 - ai2 * ai1,
                ar2 * ai1 + ai2 * ar1,
                ar2 * br1 - ai2 * bi1 + br2,
                ar2 * bi1 + ai2 * br1 + bi2)

    _, _, s_re, s_im = lax.associative_scan(
        combine, (lam_bar_re, lam_bar_im, bu_re, bu_im), axis=1)
    y = (jnp.einsum('btgn,gpn->btgp', s_re, c_re.astype(f32))
         - jnp.einsum('btgn,gpn->btgp', s_im, c_im.astype(f32))
         + d_skip.astype(f32) * u)
    y = jax.nn.gelu(y.reshape(bsz, T, S5_WIDTH))
    return (y @ w_glu_a.astype(f32)) * jax.nn.sigmoid(y @ w_glu_b.astype(f32))

def chunked_gated_delta_rule(q, k, v, g, beta):
    bsz, T, H, dk = q.shape
    dv = v.shape[-1]
    C = DN_CHUNK
    n = T // C
    q = q * (dk ** -0.5)

    def to_chunks(t):
        return t.reshape(bsz, n, C, H, -1).transpose(0, 3, 1, 2, 4)

    q, k, v = to_chunks(q), to_chunks(k), to_chunks(v)
    g = g.reshape(bsz, n, C, H).transpose(0, 3, 1, 2)
    beta = beta.reshape(bsz, n, C, H).transpose(0, 3, 1, 2)
    g = jnp.cumsum(g, axis=-1)
    incl = jnp.tril(jnp.ones((C, C), dtype=bool))
    strict = jnp.tril(jnp.ones((C, C), dtype=bool), -1)
    decay = jnp.exp(jnp.where(incl, g[..., :, None] - g[..., None, :], -jnp.inf))
    kb = k * beta[..., None]
    a_mat = jnp.where(strict, jnp.einsum('bhncd,bhnsd->bhncs', kb, k) * decay, 0.0)
    lower = a_mat + jnp.eye(C, dtype=a_mat.dtype)
    rhs = jnp.concatenate([v * beta[..., None], kb * jnp.exp(g)[..., None]], axis=-1)
    sol = lax.linalg.triangular_solve(lower, rhs, left_side=True, lower=True, unit_diagonal=True)
    u_chunk = sol[..., :dv]
    w_chunk = sol[..., dv:]
    attn_intra = jnp.where(incl, jnp.einsum('bhncd,bhnsd->bhncs', q, k) * decay, 0.0)
    q_dec = q * jnp.exp(g)[..., None]
    k_dec = k * jnp.exp(g[..., -1:] - g)[..., None]
    g_last = jnp.exp(g[..., -1])

    def step(S, xs):
        qd, wc, uc, at, kd, gl = xs
        v_new = uc - jnp.einsum('bhcd,bhde->bhce', wc, S)
        o = jnp.einsum('bhcd,bhde->bhce', qd, S) + jnp.einsum('bhcs,bhse->bhce', at, v_new)
        S = S * gl[..., None, None] + jnp.einsum('bhcd,bhce->bhde', kd, v_new)
        return S, o

    xs = (jnp.moveaxis(q_dec, 2, 0), jnp.moveaxis(w_chunk, 2, 0), jnp.moveaxis(u_chunk, 2, 0),
          jnp.moveaxis(attn_intra, 2, 0), jnp.moveaxis(k_dec, 2, 0), jnp.moveaxis(g_last, 2, 0))
    S0 = jnp.zeros((bsz, H, dk, dv), jnp.float32)
    _, o = lax.scan(step, S0, xs)
    return o.transpose(1, 0, 3, 2, 4).reshape(bsz, T, H, dv)

def deltanet_branch(qkv, z, beta_logit, decay_logit, conv_w, a_log, dt_bias, norm_w, w_dn_out):
    f32 = jnp.float32
    bsz, T, _ = qkv.shape
    qkv = jax.nn.silu(causal_depthwise_conv(qkv.astype(f32), conv_w.astype(f32)))
    q = l2_normalize(qkv[..., :DN_KEY_WIDTH].reshape(bsz, T, DN_QK_HEADS, DN_HEAD_DIM))
    k = l2_normalize(qkv[..., DN_KEY_WIDTH:2 * DN_KEY_WIDTH].reshape(bsz, T, DN_QK_HEADS, DN_HEAD_DIM))
    v = qkv[..., 2 * DN_KEY_WIDTH:].reshape(bsz, T, DN_V_HEADS, DN_HEAD_DIM)
    rep = DN_V_HEADS // DN_QK_HEADS
    q = jnp.repeat(q, rep, axis=2)
    k = jnp.repeat(k, rep, axis=2)
    beta = jax.nn.sigmoid(beta_logit.astype(f32))
    g = -jnp.exp(a_log.astype(f32)) * jax.nn.softplus(decay_logit.astype(f32) + dt_bias.astype(f32))
    o = chunked_gated_delta_rule(q, k, v, g, beta)
    o = o * lax.rsqrt(jnp.mean(jnp.square(o), axis=-1, keepdims=True) + RMS_EPS)
    o = o * norm_w.astype(f32) * jax.nn.silu(z.astype(f32).reshape(bsz, T, DN_V_HEADS, DN_HEAD_DIM))
    return o.reshape(bsz, T, DN_VALUE_WIDTH) @ w_dn_out.astype(f32)

def token_mixer(x, w_in, dn_conv_w, dn_a_log, dn_dt_bias, dn_norm_w, w_dn_out,
                s5_lam_re, s5_lam_im, s5_log_dt, s5_b_re, s5_b_im, s5_c_re, s5_c_im, s5_d,
                w_glu_a, w_glu_b, w_mix_out):
    proj = x @ w_in
    y_s5 = s5_branch(proj[..., OFF_S5:OFF_QKV], s5_lam_re, s5_lam_im, s5_log_dt,
                     s5_b_re, s5_b_im, s5_c_re, s5_c_im, s5_d, w_glu_a, w_glu_b)
    y_dn = deltanet_branch(proj[..., OFF_QKV:OFF_Z], proj[..., OFF_Z:OFF_BETA],
                           proj[..., OFF_BETA:OFF_DECAY], proj[..., OFF_DECAY:OFF_GATE_S5],
                           dn_conv_w, dn_a_log, dn_dt_bias, dn_norm_w, w_dn_out)
    gate_s5 = jax.nn.sigmoid(proj[..., OFF_GATE_S5:OFF_GATE_DN].astype(jnp.float32))
    gate_dn = jax.nn.sigmoid(proj[..., OFF_GATE_DN:IN_COLS].astype(jnp.float32))
    merged = gate_s5 * y_s5 + gate_dn * y_dn
    return (merged @ w_mix_out.astype(jnp.float32)).astype(x.dtype)

def routed_experts(x, w_router, b_router, w_gate, b_gate, w_up, b_up, w_down, b_down):
    bsz, T_seq, D = x.shape
    T = bsz * T_seq
    x2 = x.reshape(T, D)
    logits = x2.astype(jnp.float32) @ w_router.astype(jnp.float32) + b_router.astype(jnp.float32)
    top_val, top_idx = lax.top_k(logits, TOP_K)
    top_w = jax.nn.softmax(top_val, axis=-1)
    TK = T * TOP_K
    flat_e = top_idx.reshape(-1)
    flat_tok = jnp.repeat(jnp.arange(T, dtype=jnp.int32), TOP_K)
    flat_w = top_w.reshape(-1)
    order = jnp.argsort(flat_e)
    se, stok, sw = flat_e[order], flat_tok[order], flat_w[order]
    counts = jnp.bincount(flat_e, length=N_EXPERTS)
    padded = (counts + MOE_BLOCK - 1) // MOE_BLOCK * MOE_BLOCK
    start = jnp.cumsum(counts) - counts
    pend = jnp.cumsum(padded)
    pstart = pend - padded
    dest = pstart[se] + (jnp.arange(TK, dtype=jnp.int32) - start[se])
    n_blocks = -(-TK // MOE_BLOCK) + N_EXPERTS
    n_slots = n_blocks * MOE_BLOCK
    slot_tok = jnp.full((n_slots,), T, jnp.int32).at[dest].set(stok)
    slot_w = jnp.zeros((n_slots,), jnp.float32).at[dest].set(sw)
    block_e = jnp.minimum(jnp.searchsorted(pend, jnp.arange(n_blocks, dtype=jnp.int32) * MOE_BLOCK,
                                           side='right'), N_EXPERTS - 1)
    x_pad = jnp.concatenate([x2, jnp.zeros((1, D), x2.dtype)], axis=0)

    def expert_block(args):
        tok, e = args
        xb = x_pad[tok]
        gate = jnp.minimum(xb @ w_gate[e] + b_gate[e], SWIGLU_LIMIT)
        up = jnp.clip(xb @ w_up[e] + b_up[e], -SWIGLU_LIMIT, SWIGLU_LIMIT)
        h = gate * jax.nn.sigmoid(SWIGLU_ALPHA * gate) * (up + 1.0)
        return h @ w_down[e] + b_down[e]

    y = lax.map(expert_block, (slot_tok.reshape(n_blocks, MOE_BLOCK), block_e))
    y = y.reshape(n_slots, D) * slot_w[:, None]
    out = jax.ops.segment_sum(y, slot_tok, num_segments=T + 1)[:T]
    return out.reshape(bsz, T_seq, D).astype(x.dtype)

def setup_inputs(seed: int = 0) -> dict:
    key = jax.random.key(seed)
    ks = jax.random.split(key, 32)
    f32 = jnp.float32
    L, D = DEPTH, D_MODEL

    def normal(k, shape, scale):
        return jax.random.normal(k, shape, f32) * scale

    def uniform(k, shape, lo, hi):
        return jax.random.uniform(k, shape, f32, lo, hi)

    x = normal(ks[0], (BATCH, SEQ, D), 1.0)
    w_in = normal(ks[1], (L, D, IN_COLS), D ** -0.5)
    dn_conv_w = normal(ks[2], (L, DN_CONV_CH, DN_CONV), DN_CONV ** -0.5)
    dn_a_log = jnp.log(uniform(ks[3], (L, DN_V_HEADS), 1.0, 16.0))
    dn_dt = jnp.exp(uniform(ks[4], (L, DN_V_HEADS), math.log(DT_MIN), math.log(DT_MAX)))
    dn_dt_bias = dn_dt + jnp.log(-jnp.expm1(-dn_dt))
    dn_norm_w = 1.0 + normal(ks[5], (L, DN_HEAD_DIM), 0.02)
    w_dn_out = normal(ks[6], (L, DN_VALUE_WIDTH, D), DN_VALUE_WIDTH ** -0.5)
    s5_lam_re = -0.5 + normal(ks[7], (L, S5_GROUPS, S5_STATE), 0.01)
    s5_lam_im = math.pi * jnp.arange(S5_STATE, dtype=f32) + normal(ks[8], (L, S5_GROUPS, S5_STATE), 0.01)
    s5_log_dt = uniform(ks[9], (L, S5_GROUPS), math.log(DT_MIN), math.log(DT_MAX))
    s5_b_re = normal(ks[10], (L, S5_GROUPS, S5_STATE, S5_GROUP_CH), (2 * S5_GROUP_CH) ** -0.5)
    s5_b_im = normal(ks[11], (L, S5_GROUPS, S5_STATE, S5_GROUP_CH), (2 * S5_GROUP_CH) ** -0.5)
    s5_c_re = normal(ks[12], (L, S5_GROUPS, S5_GROUP_CH, S5_STATE), S5_STATE ** -0.5)
    s5_c_im = normal(ks[13], (L, S5_GROUPS, S5_GROUP_CH, S5_STATE), S5_STATE ** -0.5)
    s5_d = normal(ks[14], (L, S5_GROUPS, S5_GROUP_CH), 1.0)
    w_glu_a = normal(ks[15], (L, S5_WIDTH, D), S5_WIDTH ** -0.5)
    w_glu_b = normal(ks[16], (L, S5_WIDTH, D), S5_WIDTH ** -0.5)
    w_mix_out = normal(ks[17], (L, D, D), D ** -0.5 * DEEPNORM_BETA)
    ln1_g = 1.0 + normal(ks[18], (L, D), 0.02)
    ln1_b = normal(ks[19], (L, D), 0.02)
    w_router = normal(ks[20], (L, D, N_EXPERTS), D ** -0.5)
    b_router = normal(ks[21], (L, N_EXPERTS), 0.01)
    w_gate = normal(ks[22], (L, N_EXPERTS, D, D_EXPERT), D ** -0.5)
    b_gate = normal(ks[23], (L, N_EXPERTS, D_EXPERT), 0.02)
    w_up = normal(ks[24], (L, N_EXPERTS, D, D_EXPERT), D ** -0.5)
    b_up = normal(ks[25], (L, N_EXPERTS, D_EXPERT), 0.02)
    w_down = normal(ks[26], (L, N_EXPERTS, D_EXPERT, D), D_EXPERT ** -0.5 * DEEPNORM_BETA)
    b_down = normal(ks[27], (L, N_EXPERTS, D), 0.02)
    ln2_g = 1.0 + normal(ks[28], (L, D), 0.02)
    ln2_b = normal(ks[29], (L, D), 0.02)
    return {'x': x, 'w_in': w_in, 'dn_conv_w': dn_conv_w, 'dn_a_log': dn_a_log,
            'dn_dt_bias': dn_dt_bias, 'dn_norm_w': dn_norm_w, 'w_dn_out': w_dn_out,
            's5_lam_re': s5_lam_re, 's5_lam_im': s5_lam_im, 's5_log_dt': s5_log_dt,
            's5_b_re': s5_b_re, 's5_b_im': s5_b_im, 's5_c_re': s5_c_re, 's5_c_im': s5_c_im,
            's5_d': s5_d, 'w_glu_a': w_glu_a, 'w_glu_b': w_glu_b, 'w_mix_out': w_mix_out,
            'ln1_g': ln1_g, 'ln1_b': ln1_b, 'w_router': w_router, 'b_router': b_router,
            'w_gate': w_gate, 'b_gate': b_gate, 'w_up': w_up, 'b_up': b_up,
            'w_down': w_down, 'b_down': b_down, 'ln2_g': ln2_g, 'ln2_b': ln2_b}

def reference(x, w_in, dn_conv_w, dn_a_log, dn_dt_bias, dn_norm_w, w_dn_out,
              s5_lam_re, s5_lam_im, s5_log_dt, s5_b_re, s5_b_im, s5_c_re, s5_c_im, s5_d,
              w_glu_a, w_glu_b, w_mix_out, ln1_g, ln1_b, w_router, b_router,
              w_gate, b_gate, w_up, b_up, w_down, b_down, ln2_g, ln2_b):
    h = x
    for l in range(DEPTH):
        mix = token_mixer(h, w_in[l], dn_conv_w[l], dn_a_log[l], dn_dt_bias[l], dn_norm_w[l], w_dn_out[l],
                          s5_lam_re[l], s5_lam_im[l], s5_log_dt[l], s5_b_re[l], s5_b_im[l],
                          s5_c_re[l], s5_c_im[l], s5_d[l], w_glu_a[l], w_glu_b[l], w_mix_out[l])
        h = layer_norm(DEEPNORM_ALPHA * h + mix, ln1_g[l], ln1_b[l])
        ffn = routed_experts(h, w_router[l], b_router[l], w_gate[l], b_gate[l], w_up[l], b_up[l],
                             w_down[l], b_down[l])
        h = layer_norm(DEEPNORM_ALPHA * h + ffn, ln2_g[l], ln2_b[l])
    return h


_drawn_inputs = setup_inputs


def setup_inputs(seed=0):
    import zlib

    import numpy as np

    out = dict(_drawn_inputs(seed))
    spreads = {}
    factors = {'dn_norm_w': 5.195,
     's5_lam_re': 64.0,
     's5_lam_im': 17.291,
     's5_log_dt': 19.44,
     's5_b_re': 36.12,
     's5_b_im': 27.488,
     's5_c_re': 33.072,
     's5_c_im': 26.808,
     'b_router': 3.842,
     'b_gate': 8.0,
     'b_up': 8.0,
     'b_down': 6.417,
     'ln2_g': 7.476,
     'ln2_b': 7.796}
    for name, (base, spread) in spreads.items():
        noise = np.random.default_rng([zlib.crc32(name.encode()), seed]).standard_normal(out[name].shape)
        drawn = base * np.exp(spread * noise) if base else spread * noise
        out[name] = jnp.asarray(drawn.astype(out[name].dtype))
    for name, factor in factors.items():
        out[name] = (out[name] * factor).astype(out[name].dtype)
    return out
```

```python
import math
from contextlib import ExitStack

import concourse.bass as bass
from concourse import mybir

ALU = mybir.AluOpType
ACT = mybir.ActivationFunctionType
F32 = mybir.dt.float32
I32 = mybir.dt.int32
AX_X = mybir.AxisListType.X

P = 128
T = 256
MT = T // P
D = 2048
KD = D // P
SC = 256
RING = 3
H_V, H_QK = 32, 16
GROUPS = 8
GV, GQ = H_V // GROUPS, H_QK // GROUPS
LEVELS = 7
OFF_Q = 2048
OFF_K = OFF_Q + H_QK * P
OFF_V = OFF_K + H_QK * P
OFF_Z = OFF_V + H_V * P
OFF_BD = OFF_Z + H_V * P
OFF_GS5 = OFF_BD + 2 * H_V
OFF_GDN = OFF_GS5 + D
STEPS = 64
NCH = T // STEPS
NJ = 64
N_E, TOP_K, F_E = 32, 4, 512
KF = F_E // P
ALPHA = 2.0 ** 0.25
LIMIT, SW_ALPHA = 7.0, 1.702
LN_EPS, RMS_EPS, L2_EPS = 1e-5, 1e-6, 1e-6
TWO_PI = 2.0 * math.pi
TWO_PI_HI = 6.28125
TWO_PI_LO = TWO_PI - TWO_PI_HI
PI_SAFE = 3.1415925

S_GROUP = 0
S_U = S_GROUP + 6 * GROUPS
S_DN = S_U + 8
S_GLU = S_DN + 24
S_MIX = S_GLU + 24
U_USE = 2 * GROUPS
DN_USE = U_USE + 3
GLU_USE = DN_USE + 8
GS5_USE = U_USE + 2
MIX_USE = (GLU_USE + 8, GLU_USE + 8, GS5_USE + 8)


def build(nc, x, w_in, conv_w, a_log, dt_bias, norm_w, w_dn, lam_re, lam_im, log_dt, b_re, b_im, c_re, c_im,
          d_skip, w_glu_a, w_glu_b, w_mix, ln1_g, ln1_b, w_router, b_router, w_gate, b_gate, w_up, b_up,
          w_down, b_down, ln2_g, ln2_b, out):
    ds = bass.ds
    with ExitStack() as ctx:
        def sb(name, shape, dt=F32):
            return ctx.enter_context(nc.sbuf_tensor(name, shape, dt))

        def sem(name):
            return ctx.enter_context(nc.semaphore(name))

        ps = [ctx.enter_context(nc.psum_tensor(f"bank{i}", [P, 512], F32)) for i in range(8)]
        ident = sb("ident", [P, P])
        masks = sb("masks", [P, 8 * P])
        upper = masks[:, 0:P]
        ones = sb("ones", [P, P])
        level_mask = masks[:, P:8 * P].rearrange("p (l t) -> p l t", l=LEVELS)
        uch = masks[:, :].rearrange("p (k t) -> p k t", k=KD)
        cw = sb("cw", [P, 64, 4])
        small = sb("small", [P, 448])
        beta = small[:, 0:64].rearrange("p (c h) -> p c h", c=2)
        gcum = small[:, 64:128].rearrange("p (c h) -> p c h", c=2)
        glog = small[:, 128:192].rearrange("p (c h) -> p c h", c=2)
        neg_eg = small[:, 192:224]
        kd = small[:, 224:256]
        arow = small[:, 256:288]
        dtrow = small[:, 288:320]
        normw = small[:, 320:321]
        dsk = small[:, 321:337]
        stats = small[:, 340:396]
        eps_ln = small[:, 396:397]
        eps_l2 = small[:, 397:398]
        lnq = small[:, 398:399]
        zero1 = small[:, 399:400]
        halfmask = small[:, 400:402]
        ggrp = small[:, 402:410].rearrange("p (c a) -> p c a", c=2)
        itmp = sb("itmp", [P, NJ], I32)

        ARENA = 51000
        arena = sb("arena", [P, ARENA])

        def at(off, *dims):
            n = 1
            for d in dims:
                n *= d
            assert off + n <= ARENA, (off, dims)
            v = arena[:, off:off + n]
            if len(dims) == 1:
                return v
            names = "abcde"[:len(dims)]
            return v.rearrange(f"p ({' '.join(names)}) -> p {' '.join(names)}",
                               **{names[i]: dims[i] for i in range(1, len(dims))})

        ring = at(0, RING, KD, SC)
        XT = 12288
        xT = at(XT, KD, T)
        OT = 16384
        oT = at(OT, H_V, T)
        SH = 24576
        xtok = at(SH, MT, D)
        wbd = at(SH + 4096, KD, 2 * H_V)
        sp0 = at(SH + 5120, 2, 2, 32)
        qkT = at(SH, 2, GQ, T)
        ktok = at(SH + 1024, GQ, P)
        vtok = at(SH + 1280, 2, GV, P)
        cv = at(SH + 2304, 2, 512)
        sq = at(SH + 3328, 1024)
        rn = at(SH + 4352, 1024)
        Eg = at(SH + 5376, GV, P)
        kdec = at(SH + 5888, GV, P)
        vn = at(SH + 6400, 2, GV, P)
        Sst = at(SH + 7424, GV, P)
        R = at(SH + 7936, GV, P)
        qd = at(SH + 8448, GV, P)
        zs = at(SH + 8960, GV, T)
        w0 = SH + 9984
        gU = at(w0, 2, GV, P)
        Dc = at(w0 + 1024, 2, GV, P)
        Dm = at(w0 + 2048, 2, GV, P)
        At = at(w0 + 3072, 2, GV, P)
        attn = at(w0 + 4096, 2, GV, P)
        Ti = at(w0 + 5120, 2, GV, P)
        Tt = at(w0 + 6144, 2, GV, P)
        Pm = at(w0 + 7168, 2, GV, P)
        zvT = at(w0 + 8192, GV, T)
        uT = at(SH, KD, T)
        SS0 = SH + 4096
        SS = at(SS0, STEPS + 1, 2, NJ)
        BT0 = SS0 + (STEPS + 1) * 2 * NJ
        BT = at(BT0, 2, KD, P)
        CT = at(BT0 + 4096, 2, KD, P)
        MG = BT0 + 8192
        mg = at(MG, KD, T)
        TM = MG + 4096
        Arr = at(TM, 2, NJ)
        Aim = at(TM + 128, 2, NJ)
        m1 = at(TM + 256, 2, NJ)
        m2 = at(TM + 384, 2, NJ)
        gdt = at(TM + 512, 512)
        ytmp = at(TM + 1024, 8, STEPS)
        spar = at(MG, 3, P)
        coef = at(MG + 384, 16, NJ)
        braw = at(SS0 + 128, 2, NJ, 16)
        bb = at(SS0 + 128 + 2048, 2, NJ, 16)
        bt1 = at(SS0 + 128 + 4096, NJ, 16)
        craw = at(MG + 2048, 2, KD, 64)
        bwide = at(BT0 + 4096, 2, NJ, 32)
        cwide = at(SS0 + 128, 2, KD, 2, 64)
        ta = at(TM + 512, 512)
        tb = at(TM + 1024, 512)
        h1 = at(SH, MT, D)
        acc = at(SH + 4096, MT, D)
        lnrow = at(XT, 2, D)
        h1T = at(XT, KD, T)
        GW = at(SH + 8192, KD, F_E)
        UW = at(SH + 16384, KD, F_E)
        DW = at(OT, KF, D)
        bdn = at(0, D)
        gb = at(2048, MT, F_E)
        sg = at(3072, MT, F_E)
        hb = at(4096, MT, F_E)
        hT = at(5120, KF, T)
        brow = at(6144, 2, F_E)
        wr = at(7168, KD, N_E)
        ln2row = at(8192, 2, D)
        rt = at(TM, 8, MT, N_E)
        wt = rt[:, 0]
        rm = sb("rm", [P, 8, MT])
        wtT = at(TM + 512, T)[0:N_E]

        const_ready = sem("const_ready")
        load_free, scan_begun = sem("load_free"), sem("scan_begun")
        pro_loaded = sem("pro_loaded")
        slot_loaded = [sem(f"slot{i}_loaded") for i in range(RING)]
        bank_ready = [sem(f"bank{i}_ready") for i in range(3)]
        bank_taken = [sem(f"bank{i}_taken") for i in range(3)]
        xt_ready, xt_taken = sem("xt_ready"), sem("xt_taken")
        bd_ready, glog_ready, gcum_ready, prologue_done = (sem("bd_ready"), sem("glog_ready"), sem("gcum_ready"),
                                                           sem("prologue_done"))
        sp_in, sp_done, kd_in, kd_out = sem("sp_in"), sem("sp_done"), sem("kd_in"), sem("kd_out")
        s5_dve, s5_act, ln_act, rev_ready = sem("s5_dve"), sem("s5_act"), sem("ln_act"), sem("rev_ready")
        conv_ready, conv_taken = sem("conv_ready"), sem("conv_taken")
        sq_ready, ss_ready, rn_ready, qk_ready = sem("sq_ready"), sem("ss_ready"), sem("rn_ready"), sem("qk_ready")
        tok_ready, tok_taken, vtok_taken = sem("tok_ready"), sem("tok_taken"), sem("vtok_taken")
        gu_ready, gb_ready, arg_ready, dexp_ready, dm_ready = (sem("gu_ready"), sem("gb_ready"), sem("arg_ready"),
                                                              sem("dexp_ready"), sem("dm_ready"))
        kq_ready, aux_ready = sem("kq_ready"), sem("aux_ready")
        t_ready = [sem(f"t{c}_ready") for c in range(2)]
        p_ready = [sem(f"p{c}_ready") for c in range(2)]
        pm_ready = [sem(f"pm{c}_ready") for c in range(2)]
        x_ready = [sem(f"x{c}_ready") for c in range(2)]
        apply_pe, apply_dve, apply_act = sem("apply_pe"), sem("apply_dve"), sem("apply_act")
        osq_ready, oss_ready, orn_ready, o_ready = sem("osq_ready"), sem("oss_ready"), sem("orn_ready"), sem("o_ready")
        z_ready = sem("z_ready")
        phase_done = [sem(f"phase{i}_done") for i in range(5)]
        s5_loaded, s5_tr, s5_trc, s5_step = sem("s5_loaded"), sem("s5_tr"), sem("s5_trc"), sem("s5_step")
        uch_ready = sem("uch_ready")
        bu_ready, bu_taken, chunk_filled, scan_done = (sem("bu_ready"), sem("bu_taken"), sem("chunk_filled"),
                                                       sem("scan_done"))
        y_ready, y_taken, gd_ready, merged_ready = sem("y_ready"), sem("y_taken"), sem("gd_ready"), sem("merged_ready")
        gelu_done = sem("gelu_done")
        glu_ready, glu_used = sem("glu_ready"), sem("glu_used")
        x_loaded, ln_loaded, ln_step = sem("x_loaded"), sem("ln_loaded"), sem("ln_step")
        h1_ready, ht_ready, ht_taken, logit_ready, wt_ready, wtt_ready, wtt_taken = (
            sem("h1_ready"), sem("ht_ready"), sem("ht_taken"), sem("logit_ready"), sem("wt_ready"),
            sem("wtt_ready"), sem("wtt_taken"))
        rt_loaded, rexp_in, rexp_out = sem("rt_loaded"), sem("rexp_in"), sem("rexp_out")
        bd2_ready, acc0_ready = sem("bd2_ready"), sem("acc0_ready")
        gw_loaded, uw_loaded, dw_loaded, brow_loaded = (sem("gw_loaded"), sem("uw_loaded"), sem("dw_loaded"),
                                                        sem("brow_loaded"))
        gate_done, gate_taken, up_done, up_taken = sem("gate_done"), sem("gate_taken"), sem("up_done"), sem("up_taken")
        sig_ready, hb_ready = sem("sig_ready"), sem("hb_ready")
        htr_ready, htr_taken = sem("htr_ready"), sem("htr_taken")
        dn_ready = [sem(f"down_bank{i}_ready") for i in range(2)]
        dn_taken = [sem(f"down_bank{i}_taken") for i in range(2)]
        ln2_loaded, out_ready, out_done = sem("ln2_loaded"), sem("out_ready"), sem("out_done")

        def in_rows(w):
            return w.rearrange("(p k) n -> p k n", k=KD)

        def tile_rows(w):
            return w.rearrange("(k p) n -> p k n", p=P)

        block = ctx.enter_context(nc.Block())

        @block.sync
        def _(sp):
            sp.dma_start(xtok, x[0].rearrange("(m p) d -> p m d", p=P)).then_inc(pro_loaded, 16)
            sp.dma_start(wbd, in_rows(w_in[:, OFF_BD:OFF_BD + 2 * H_V])).then_inc(pro_loaded, 16)
            sp.dma_start(cw[:, :, :], conv_w.rearrange("(j p) t -> p j t", p=P)).then_inc(pro_loaded, 16)
            sp.dma_start(arow, a_log.partition_broadcast(P)).then_inc(pro_loaded, 16)
            sp.dma_start(dtrow, dt_bias.partition_broadcast(P)).then_inc(pro_loaded, 16)
            sp.dma_start(normw, norm_w.rearrange("(p o) -> p o", o=1)).then_inc(pro_loaded, 16)

            def load_slot(buf, src, bank, taken):
                sp.wait_ge(bank_taken[bank], taken)
                sp.sem_inc(load_free, 1)
                sp.dma_start(ring[:, buf], src).then_inc(slot_loaded[buf], 16)

            with sp.Fori(0, GROUPS) as g:
                for r, col in enumerate((OFF_Q + 256 * g, OFF_K + 256 * g, OFF_V + 512 * g, OFF_V + 256 + 512 * g,
                                         OFF_Z + 512 * g, OFF_Z + 256 + 512 * g)):
                    load_slot(r % RING, in_rows(w_in[:, ds(col, SC)]), r % 3, 2 * g + r // 3 + 1)
            sp.wait_ge(phase_done[0], 4)
            sp.dma_start(spar[0:NJ, 0, :], lam_re.rearrange("(j g) n -> j (g n)", g=2)).then_inc(s5_loaded, 16)
            sp.dma_start(spar[0:NJ, 1, :], lam_im.rearrange("(j g) n -> j (g n)", g=2)).then_inc(s5_loaded, 16)
            sp.dma_start(coef[0:NJ, 15, 0:2], log_dt.rearrange("(j g) -> j g", g=2)).then_inc(s5_loaded, 16)
            for c, b in enumerate((b_re, b_im)):
                bv = b.rearrange("(j g) n q -> g n j q", g=2)
                for g2 in range(2):
                    sp.dma_start(braw[64 * g2:64 * g2 + 64, c], bv[g2]).then_inc(s5_loaded, 16)
            for c, cc in enumerate((c_re, c_im)):
                sp.dma_start(craw[:, c], cc.rearrange("(k a) q n -> (a q) k n", k=KD)).then_inc(s5_loaded, 16)
            sp.dma_start(dsk, d_skip.rearrange("(k a) q -> (a q) k", k=KD), allow_slow_non_contiguous=True).then_inc(s5_loaded, 16)
            with sp.Fori(0, 2) as q:
                for r in range(3):
                    load_slot((S_U + r) % RING, in_rows(w_in[:, ds(768 * q + 256 * r, SC)]), r, U_USE + q + 1)
            for r in range(6, 8):
                load_slot((S_U + r) % RING, in_rows(w_in[:, SC * r:SC * r + SC]), r % 3, U_USE + 3)
            with sp.Fori(0, 8) as c:
                load_slot(S_DN % RING, in_rows(w_in[:, ds(OFF_GDN + SC * c, SC)]), 0, DN_USE + 1 + c)
                for h in range(2):
                    load_slot((S_DN + 1 + h) % RING, tile_rows(w_dn[h * D:h * D + D, ds(SC * c, SC)]), 1,
                              DN_USE + 1 + c)
            with sp.Fori(0, 8) as c:
                load_slot(S_GLU % RING, tile_rows(w_glu_a[:, ds(SC * c, SC)]), 0, GLU_USE + 1 + c)
                load_slot((S_GLU + 1) % RING, tile_rows(w_glu_b[:, ds(SC * c, SC)]), 1, GLU_USE + 1 + c)
                load_slot((S_GLU + 2) % RING, in_rows(w_in[:, ds(OFF_GS5 + SC * c, SC)]), 2, GS5_USE + 1 + c)
            load_slot(S_MIX % RING, tile_rows(w_mix[:, 0:SC]), 0, MIX_USE[0] + 1)
            sp.wait_ge(phase_done[2], 4)
            sp.dma_start(h1, x[0].rearrange("(m p) d -> p m d", p=P)).then_inc(x_loaded, 16)
            sp.dma_start(lnrow[:, 0], ln1_g.partition_broadcast(P)).then_inc(ln_loaded, 16)
            sp.dma_start(lnrow[:, 1], ln1_b.partition_broadcast(P)).then_inc(ln_loaded, 16)
            for r in range(1, 2):
                load_slot((S_MIX + r) % RING, tile_rows(w_mix[:, SC * r:SC * r + SC]), r, MIX_USE[r] + 1)
            with sp.Fori(0, 2) as q:
                for r in range(2, 5):
                    load_slot((S_MIX + r) % RING, tile_rows(w_mix[:, ds(768 * q + SC * r, SC)]), r % 3,
                              MIX_USE[r % 3] + r // 3 + 1 + q)

            def load_gate(e):
                sp.dma_start(GW.rearrange("p k n -> p (k n)"),
                             w_gate[ds(e, 1)].rearrange("o (p k) n -> p (o k n)", k=KD)).then_inc(gw_loaded, 16)

            def load_up(e):
                sp.dma_start(brow[:, 0], b_gate[ds(e, 1)].rearrange("o n -> (o n)").partition_broadcast(P)).then_inc(brow_loaded, 16)
                sp.dma_start(brow[:, 1], b_up[ds(e, 1)].rearrange("o n -> (o n)").partition_broadcast(P)).then_inc(brow_loaded, 16)
                sp.dma_start(UW.rearrange("p k n -> p (k n)"),
                             w_up[ds(e, 1)].rearrange("o (p k) n -> p (o k n)", k=KD)).then_inc(uw_loaded, 16)

            def load_down(e):
                sp.dma_start(DW.rearrange("p k n -> p (k n)"),
                             w_down[ds(e, 1)].rearrange("o (p k) n -> p (o k n)", k=KF)).then_inc(dw_loaded, 16)

            load_gate(0)
            sp.wait_ge(phase_done[3], 4)
            sp.dma_start(wr, w_router.rearrange("(p k) e -> p k e", k=KD)).then_inc(rt_loaded, 16)
            sp.dma_start(rt[:, 7, 0], b_router.partition_broadcast(P)).then_inc(rt_loaded, 16)
            sp.dma_start(rt[:, 7, 1], b_router.partition_broadcast(P)).then_inc(rt_loaded, 16)
            sp.dma_start(bdn[0:N_E, :], b_down).then_inc(rt_loaded, 16)
            load_up(0)
            sp.dma_start(ln2row[:, 0], ln2_g.partition_broadcast(P)).then_inc(ln2_loaded, 16)
            sp.dma_start(ln2row[:, 1], ln2_b.partition_broadcast(P)).then_inc(ln2_loaded, 16)
            with sp.Fori(0, N_E - 1) as e:
                sp.wait_ge(gate_done, e + 1)
                sp.sem_inc(load_free, 1)
                load_gate(e + 1)
                sp.wait_ge(dn_taken[1], 4 * e + 1)
                sp.sem_inc(load_free, 1)
                load_down(e)
                sp.wait_ge(up_taken, 2 * e + 2)
                sp.sem_inc(load_free, 1)
                load_up(e + 1)
            sp.wait_ge(dn_taken[1], 4 * N_E - 3)
            load_down(N_E - 1)
            for m in range(MT):
                sp.wait_ge(out_ready, m + 1)
                sp.dma_start(out[0, m * P:m * P + P, :], h1[:, m]).then_inc(out_done, 16)
            sp.wait_ge(out_done, 32)

        @block.gpsimd
        def _(pool):
            g = nc.gpsimd
            g.memset(ident[:, :], 0.0)
            g.memset(upper, 1.0)
            g.memset(ones[:, :], 1.0)
            g.memset(level_mask, 0.0)
            g.memset(eps_ln, LN_EPS)
            g.memset(eps_l2, L2_EPS)
            g.memset(zero1, 0.0)
            g.memset(lnq, -0.5 * math.log(P))
            g.memset(halfmask, 1.0)
            pool.drain()
            g.affine_select(out=ident[:, :], in_=ident[:, :], compare_op=ALU.not_equal, fill=1.0, base=0,
                            pattern=[[-1, P]], channel_multiplier=1)
            g.affine_select(out=upper, in_=upper, compare_op=ALU.is_ge, fill=0.0, base=0,
                            pattern=[[1, P]], channel_multiplier=-1)
            for lv in range(LEVELS):
                s = 1 << lv
                g.memset(level_mask[:, lv].rearrange("p (b h j) -> p b h j", h=2, j=s)[:, :, 0, :], 1.0)
            pool.drain()
            for lv in range(LEVELS):
                s = 1 << lv
                v = level_mask[:, lv].rearrange("p (b j) -> p b j", j=2 * s)
                g.affine_select(out=v, in_=v, compare_op=ALU.is_ge, fill=0.0, base=-s,
                                pattern=[[-2 * s, P // (2 * s)], [0, 2 * s]], channel_multiplier=1)
            pool.drain()
            for lv in range(LEVELS):
                s = 1 << lv
                v = level_mask[:, lv].rearrange("p (b j) -> p b j", j=2 * s)
                g.affine_select(out=v, in_=v, compare_op=ALU.is_ge, fill=0.0, base=2 * s - 1,
                                pattern=[[2 * s, P // (2 * s)], [0, 2 * s]], channel_multiplier=-1)
            pool.drain()
            g.tensor_copy(halfmask[:, 1:2], level_mask[:, 4, 0:1])
            for b in range(1, 4):
                pool.drain()
                g.tensor_tensor(halfmask[:, 1:2], halfmask[:, 1:2], level_mask[:, 4, 32 * b:32 * b + 1], ALU.add)
            pool.drain()
            g.tensor_scalar(halfmask[:, 0:1], halfmask[:, 1:2], -1.0, 1.0, ALU.mult, ALU.add).then_inc(const_ready, 1)

            with pool.Fori(0, GROUPS) as gi:
                for c in range(2):
                    if c == 0:
                        pool.wait_ge(prologue_done, gi + 1)
                    g.tensor_copy(ggrp[:, c], glog[:, c, ds(GV * gi, GV)])
                    pool.drain()
                    for a in range(GV):
                        g.tensor_scalar(gU[:, c, a], upper, ggrp[:, c, a:a + 1], None, ALU.mult)
                    pool.drain()
                    pool.sem_inc(gu_ready, 1)
                for m in (Ti, Tt):
                    for c in range(2):
                        g.tensor_copy(m[:, c], ident[:, :].unsqueeze(1).to_broadcast([P, GV, P]))
                for c in range(2):
                    pool.wait_ge(dexp_ready, 2 * gi + c + 1)
                    g.tensor_tensor(Dm[:, c], Dc[:, c], upper.unsqueeze(1).to_broadcast([P, GV, P]), ALU.mult)
                    pool.drain()
                    pool.sem_inc(dm_ready, 1)
                pool.wait_ge(tok_taken, gi + 1)
                kview = kdec.rearrange("p (b r) d -> p b r d", r=2)
                g.tensor_tensor(kview, ktok.unsqueeze(2).to_broadcast([P, GQ, 2, P]),
                                kd[:, ds(GV * gi, GV)].rearrange("p (b r) -> p b r", r=2).unsqueeze(3)
                                .to_broadcast([P, GQ, 2, P]), ALU.mult)
                g.tensor_tensor(qd.rearrange("p (b r) d -> p b r d", r=2),
                                qkT[:, 0, :, P:T].unsqueeze(2).to_broadcast([P, GQ, 2, P]),
                                Eg.rearrange("p (b r) d -> p b r d", r=2), ALU.mult)
                pool.drain()
                pool.sem_inc(aux_ready, 1)
            pool.sem_inc(phase_done[0], 1)

            pool.wait_ge(s5_step, 4)
            g.memset(SS[:, 0], 0.0)
            pool.drain()
            with pool.Fori(0, NCH) as ch:
                pool.wait_ge(chunk_filled, ch + 1)
                pool.sem_inc(scan_begun, 1)
                with pool.Fori(0, STEPS) as t:
                    prev = SS[:, ds(t, 1)].rearrange("p o c j -> p (o c) j")
                    cur = SS[:, ds(t + 1, 1)].rearrange("p o c j -> p (o c) j")
                    g.tensor_tensor(m1, Arr, prev, ALU.mult)
                    g.tensor_tensor(m2[:, 0], Aim[:, 0], SS[:, ds(t, 1), 1].rearrange("p o j -> p (o j)"), ALU.mult)
                    g.tensor_tensor(m2[:, 1], Aim[:, 1], SS[:, ds(t, 1), 0].rearrange("p o j -> p (o j)"), ALU.mult)
                    pool.drain()
                    g.tensor_tensor(m1, m1, m2, ALU.add)
                    pool.drain()
                    g.tensor_tensor(cur, cur, m1, ALU.add)
                    pool.drain()
                g.tensor_copy(SS[:, 0], SS[:, STEPS])
                pool.drain()
                pool.sem_inc(scan_done, 1)
            for i in (1, 2, 3):
                pool.sem_inc(phase_done[i], 1)
            pool.wait_ge(phase_done[2], 4)
            g.iota(rt[:, 4], pattern=[[0, MT], [-1, N_E]], base=N_E, channel_multiplier=0,
                   allow_small_or_imprecise_dtypes=True).then_inc(rev_ready, 1)

        @block.tensor
        def _(pe):
            mm, tr = nc.tensor.matmul, nc.tensor.transpose
            pe.wait_ge(pro_loaded, 96)
            pe.wait_ge(const_ready, 1)
            for i in range(8):
                for j in range(4):
                    k, m = 2 * i + j // 2, j % 2
                    last = tr(ps[i][:, j * P:j * P + P], xtok[:, m, k::KD], ident[:, :])
                last.then_inc(xt_ready, 1)
            pe.wait_ge(xt_taken, 8)
            for m in range(MT):
                for k in range(KD):
                    last = mm(ps[0][:, m * 64:m * 64 + 64], xT[:, k, m * P:m * P + P], wbd[:, k, :],
                              start=k == 0, stop=k == KD - 1)
            last.then_inc(bd_ready, 1)
            pe.wait_ge(glog_ready, 1)
            gl2 = small[:, 128:192]
            mm(ps[0][:, 0:64], upper, gl2, start=True, stop=True)
            mm(ps[0][:, 64:96], ones[:, :], glog[:, 0], start=True, stop=True).then_inc(gcum_ready, 1)
            pe.wait_ge(prologue_done, 1)

            def project(arrived, buf, bank, use, rhs):
                pe.wait_ge(slot_loaded[buf], arrived)
                pe.wait_ge(bank_taken[bank], use + 1)
                for ct in range(2):
                    for k in range(KD):
                        last = mm(ps[bank][:, ct * T:ct * T + T], ring[:, buf, k, ct * P:ct * P + P], rhs[:, k, :],
                                  start=k == 0, stop=k == KD - 1)
                last.then_inc(bank_ready[bank], 1)

            with pe.Fori(0, GROUPS) as g:
                for r in range(4):
                    project(16 * (2 * g + r // 3 + 1), r % RING, r % 3, 2 * g + r // 3, xT)
                pe.wait_ge(sq_ready, g + 1)
                for i in range(2):
                    last = mm(ps[3 + i][:, :], ones[:, :], sq[:, i * 512:i * 512 + 512], start=True, stop=True)
                last.then_inc(ss_ready, 1)
                project(16 * (2 * g + 2), 1, 1, 2 * g + 1, xT)
                pe.wait_ge(qk_ready, g + 1)
                for b in range(GQ):
                    tr(ps[5][:, b * P:b * P + P], qkT[:, 1, b, 0:P], ident[:, :])
                for c in range(2):
                    for a in range(GV):
                        last = tr(ps[6 + c][:, a * P:a * P + P], zvT[:, a, c * P:c * P + P], ident[:, :])
                last.then_inc(tok_ready, 1)
                project(16 * (2 * g + 2), 2, 2, 2 * g + 1, xT)
                pe.wait_ge(tok_taken, g + 1)
                pe.wait_ge(vtok_taken, g + 1)
                for c in range(2):
                    pe.wait_ge(gu_ready, 2 * g + c + 1)
                    mm(ps[3 + 2 * c][:, :], ones[:, :], gU[:, c].rearrange("p a t -> p (a t)"),
                       start=True, stop=True).then_inc(gb_ready, 1)
                    for i in range(2):
                        for b in range(GQ):
                            last = mm(ps[4 + 2 * c][:, (2 * i + b) * P:(2 * i + b) * P + P],
                                      qkT[:, 1, b, c * P:c * P + P], qkT[:, 1 - i, b, c * P:c * P + P],
                                      start=True, stop=True)
                    last.then_inc(kq_ready, 1)
                with pe.Fori(0, LEVELS) as lv:
                    for c in range(2):
                        pe.wait_ge(t_ready[c], 8 * g + lv + 1)
                        for a in range(GV):
                            last = mm(ps[3 + 2 * c][:, a * P:a * P + P], At[:, c, a], Ti[:, c, a],
                                      start=True, stop=True)
                        last.then_inc(p_ready[c], 1)
                    for c in range(2):
                        pe.wait_ge(pm_ready[c], 7 * g + lv + 1)
                        for a in range(GV):
                            mm(ps[3 + 2 * c][:, a * P:a * P + P], Tt[:, c, a], Pm[:, c, a], start=True, stop=True)
                        for a in range(GV):
                            last = mm(ps[4 + 2 * c][:, a * P:a * P + P], Pm[:, c, a], Tt[:, c, a],
                                      start=True, stop=True)
                        last.then_inc(x_ready[c], 1)
                pe.wait_ge(t_ready[0], 8 * g + 8)
                pe.wait_ge(t_ready[1], 8 * g + 8)
                for a in range(GV):
                    last = mm(ps[3][:, a * P:a * P + P], Tt[:, 0, a], vtok[:, 0, a], start=True, stop=True)
                last.then_inc(apply_pe, 1)
                pe.wait_ge(apply_dve, 3 * g + 1)
                pe.wait_ge(aux_ready, g + 1)
                for a in range(GV):
                    last = mm(ps[4][:, a * P:a * P + P], kdec[:, a], vn[:, 0, a], start=True, stop=True)
                last.then_inc(apply_pe, 1)
                for a in range(GV):
                    last = mm(ps[7][:, a * P:a * P + P], vn[:, 0, a], attn[:, 0, a], start=True, stop=True)
                last.then_inc(apply_pe, 1)
                pe.wait_ge(apply_act, 3 * g + 1)
                for a in range(GV):
                    last = mm(ps[5][:, a * P:a * P + P], qkT[:, 1, a // 2, P:T], Sst[:, a], start=True, stop=True)
                last.then_inc(apply_pe, 1)
                pe.wait_ge(apply_dve, 3 * g + 2)
                for a in range(GV):
                    last = mm(ps[3][:, a * P:a * P + P], Tt[:, 1, a], R[:, a], start=True, stop=True)
                last.then_inc(apply_pe, 1)
                pe.wait_ge(apply_dve, 3 * g + 3)
                for a in range(GV):
                    mm(ps[6][:, a * P:a * P + P], Sst[:, a], qd[:, a], start=True, stop=False)
                    last = mm(ps[6][:, a * P:a * P + P], vn[:, 1, a], attn[:, 1, a], start=False, stop=True)
                last.then_inc(apply_pe, 1)
                pe.wait_ge(osq_ready, g + 1)
                for i in range(2):
                    last = mm(ps[3 + i][:, :], ones[:, :], sq[:, i * 512:i * 512 + 512], start=True, stop=True)
                last.then_inc(oss_ready, 1)
            pe.wait_ge(o_ready, GROUPS)
            pe.sem_inc(phase_done[0], 1)
            pe.wait_ge(phase_done[0], 4)

            def u_slot(s_div, r, use):
                project(16 * (s_div + 1), (S_U + r) % RING, r % 3, use, xT)

            with pe.Fori(0, 2) as q:
                for r in range(3):
                    u_slot(S_U // RING + q, r, U_USE + q)
            for r in range(6, 8):
                u_slot((S_U + r) // RING, r, U_USE + 2)
            pe.wait_ge(s5_loaded, 16 * 10)
            pe.wait_ge(s5_step, 1)
            for i in range(3):
                last = tr(ps[3][:, i * NJ:i * NJ + NJ], spar[0:NJ, i, :], ident[0:NJ, 0:NJ])
            last.then_inc(s5_tr, 1)
            for w, (src, need) in enumerate(((bwide, 2), (cwide, 3))):
                pe.wait_ge(s5_step, need)
                for c in range(2):
                    for q4 in range(4):
                        n = w * 8 + c * 4 + q4
                        if n >= 4:
                            pe.wait_ge(s5_trc, n - 3)
                        for k in range(4 * q4, 4 * q4 + 4):
                            piece = (bwide[:, c, 4 * k:4 * k + 4, :].rearrange("p j q -> p (j q)") if w == 0
                                     else cwide[:, c, k].rearrange("p g n -> p (g n)"))
                            last = tr(ps[4 + n % 4][:, (k % 4) * P:(k % 4) * P + P], piece, ident[:, :])
                        last.then_inc(s5_tr, 1)
            pe.wait_ge(s5_trc, 16)

            with pe.Fori(0, NCH) as ch:
                pe.wait_ge(uch_ready, ch + 1)
                for c in range(2):
                    for kh in range(2):
                        pe.wait_ge(bu_taken, 4 * ch + 2 * c + kh + 1)
                        for k in range(8):
                            for i in range(4):
                                last = mm(ps[4 + i][:, k * STEPS:k * STEPS + STEPS],
                                          BT[32 * i:32 * i + 32, c, kh * 8 + k, :],
                                          uch[32 * i:32 * i + 32, kh * 8 + k, :],
                                          start=True, stop=True)
                        last.then_inc(bu_ready, 1)
                for h in range(2):
                    project(16 * ((S_DN // RING + 1) + 2 * ch + h), S_DN % RING, 0, DN_USE + 2 * ch + h, xT)
                    pe.wait_ge(bank_taken[1], DN_USE + 2 * ch + h + 1)
                    for half in range(2):
                        buf = (S_DN + 1 + half) % RING
                        pe.wait_ge(slot_loaded[buf], 16 * ((S_DN + 1 + half) // RING + 1 + 2 * ch + h))
                        for ct in range(2):
                            for k in range(KD):
                                last = mm(ps[1][:, ct * T:ct * T + T], ring[:, buf, k, ct * P:ct * P + P],
                                          oT[:, half * KD + k, :], start=half == 0 and ct == 0 and k == 0,
                                          stop=half == 1 and k == KD - 1, skip_group_check=True)
                    last.then_inc(bank_ready[1], 1)
                pe.wait_ge(scan_done, ch + 1)
                pe.wait_ge(y_taken, ch + 1)
                for k in range(KD):
                    for i in range(4):
                        for c in range(2):
                            last = mm(ps[2 + k // 8][32 * i:32 * i + 32, (k % 8) * STEPS:(k % 8) * STEPS + STEPS],
                                      CT[:, c, k, 32 * i:32 * i + 32], SS[:, 1:STEPS + 1, c, 4 * k + i],
                                      start=c == 0, stop=c == 1)
                last.then_inc(y_ready, 1)
            pe.sem_inc(phase_done[1], 1)
            pe.wait_ge(gelu_done, 1)

            with pe.Fori(0, 8) as c:
                project(16 * (S_GLU // RING + 1 + c), S_GLU % RING, 0, GLU_USE + c, uT)
                project(16 * ((S_GLU + 1) // RING + 1 + c), (S_GLU + 1) % RING, 1, GLU_USE + c, uT)
                project(16 * ((S_GLU + 2) // RING + 1 + c), (S_GLU + 2) % RING, 2, GS5_USE + c, xT)
            pe.sem_inc(phase_done[2], 1)
            pe.wait_ge(phase_done[2], 4)

            def mix_slot(s16, r, use):
                buf, bank = (S_MIX + r) % RING, 3 + r % 3
                pe.wait_ge(slot_loaded[buf], s16)
                pe.wait_ge(bank_taken[r % 3], use)
                for m in range(MT):
                    for k in range(KD):
                        last = mm(ps[bank][:, m * SC:m * SC + SC], mg[:, k, m * P:m * P + P], ring[:, buf, k, :],
                                  start=k == 0, stop=k == KD - 1)
                last.then_inc(bank_ready[r % 3], 1)

            for r in range(2):
                mix_slot(16 * ((S_MIX + r) // RING + 1), r, MIX_USE[r] + 1)
            with pe.Fori(0, 2) as q:
                for r in range(2, 5):
                    mix_slot(16 * ((S_MIX + r) // RING + 1 + q), r, (MIX_USE[r % 3] + (r // 3) + 1) + q)
            pe.sem_inc(phase_done[3], 1)

            pe.wait_ge(h1_ready, 1)
            for i in range(8):
                for j in range(4):
                    k, m = 2 * i + j // 2, j % 2
                    last = tr(ps[i][:, j * P:j * P + P], h1[:, m, k::KD], ident[:, :])
                last.then_inc(ht_ready, 1)
            pe.wait_ge(ht_taken, 8)
            pe.wait_ge(rt_loaded, 64)
            for m in range(MT):
                for k in range(KD):
                    last = mm(ps[0][:, m * N_E:m * N_E + N_E], h1T[:, k, m * P:m * P + P], wr[:, k, :],
                              start=k == 0, stop=k == KD - 1)
            last.then_inc(logit_ready, 1)
            pe.wait_ge(wt_ready, 1)
            for m in range(MT):
                last = tr(ps[1][0:N_E, m * P:m * P + P], wt[:, m], ident[:, :])
            last.then_inc(wtt_ready, 1)
            pe.wait_ge(wtt_taken, 1)
            for m in range(MT):
                for n in range(4):
                    last = mm(ps[(2 + 4 * m + n) % 8][:, :], wtT[:, m * P:m * P + P], bdn[0:N_E, n * 512:n * 512 + 512],
                              start=True, stop=True)
            last.then_inc(bd2_ready, 1)
            pe.wait_ge(acc0_ready, 1)

            def gate(e):
                pe.wait_ge(gw_loaded, 16 * e + 16)
                pe.wait_ge(gate_taken, e + 1)
                for m in range(MT):
                    for k in range(KD):
                        last = mm(ps[m][:, :], h1T[:, k, m * P:m * P + P], GW[:, k, :], start=k == 0, stop=k == KD - 1)
                last.then_inc(gate_done, 1)

            def up(e):
                pe.wait_ge(uw_loaded, 16 * e + 16)
                for m in range(MT):
                    for k in range(KD):
                        last = mm(ps[2 + m][:, :], h1T[:, k, m * P:m * P + P], UW[:, k, :],
                                  start=k == 0, stop=k == KD - 1)
                last.then_inc(up_done, 1)

            def down(e):
                pe.wait_ge(hb_ready, e + 1)
                for m in range(MT):
                    for k in range(KF):
                        last = tr(ps[4 + m][:, k * P:k * P + P], hb[:, m, k::KF], ident[:, :])
                last.then_inc(htr_ready, 1)
                pe.wait_ge(htr_taken, e + 1)
                pe.wait_ge(dw_loaded, 16 * e + 16)
                for n in range(8):
                    pe.wait_ge(dn_taken[n % 2], 4 * e + n // 2 + 1)
                    for k in range(KF):
                        last = mm(ps[6 + n % 2][:, :], hT[:, k, (n // 4) * P:(n // 4) * P + P],
                                  DW[:, k, (n % 4) * 512:(n % 4) * 512 + 512], start=k == 0, stop=k == KF - 1)
                    last.then_inc(dn_ready[n % 2], 1)

            gate(0)
            up(0)
            with pe.Fori(1, N_E) as e:
                gate(e)
                down(e - 1)
                up(e)
            down(N_E - 1)

        @block.scalar
        def _(act):
            A = nc.scalar.activation
            for i in range(0, 8, 2):
                act.wait_ge(xt_ready, i + 1)
                nc.scalar.copy(xT[:, 2 * i:2 * i + 2, :], ps[i][:, :].rearrange("p (k t) -> p k t", k=2)).then_inc(xt_taken, 1)
            act.wait_ge(bd_ready, 1)
            bd = ps[0][:, 0:128].rearrange("p (m c) -> p m c", m=2)
            act.wait_ge(sp_in, 1)
            A(beta, bd[:, :, 0:32], ACT.Sigmoid)
            A(sp0[:, 0], sp0[:, 0], ACT.Exp)
            A(arow, arow, ACT.Exp)
            act.drain()
            A(sp0[:, 0], sp0[:, 0], ACT.Ln, bias=1.0)
            act.drain()
            act.sem_inc(sp_done, 1)
            act.wait_ge(kd_in, 1)
            A(neg_eg, gcum[:, 1], ACT.Exp)
            A(kd, kd, ACT.Exp)
            act.drain()
            act.sem_inc(kd_out, 1)

            with act.Fori(0, GROUPS) as g:
                for r in range(4):
                    act.wait_ge(conv_ready, 4 * g + r + 1)
                    dst = qkT[:, r] if r < 2 else zvT[:, 2 * (r - 2):2 * (r - 2) + 2]
                    A(dst, cv[:, r % 2].rearrange("p (h t) -> p h t", h=2), ACT.Silu).then_inc(conv_taken, 1)
                act.drain()
                A(sq, qkT.rearrange("p i h t -> p (i h t)"), ACT.Square).then_inc(sq_ready, 1)
                act.wait_ge(bank_ready[1], 2 * g + 2)
                A(zs[:, 0:2], ps[1][:, :].rearrange("p (h t) -> p h t", h=2), ACT.Silu).then_inc(bank_taken[1], 1)
                act.wait_ge(ss_ready, g + 1)
                for i in range(2):
                    A(rn[:, i * 512:i * 512 + 512], ps[3 + i][:, :], ACT.Ln, bias=eps_l2)
                act.drain()
                A(rn[:, 0:512], rn[:, 0:512], ACT.Exp, scale=-0.5, bias=lnq)
                A(rn[:, 512:1024], rn[:, 512:1024], ACT.Exp, scale=-0.5).then_inc(rn_ready, 1)
                act.wait_ge(tok_ready, g + 1)
                for c in range(2):
                    last = nc.scalar.copy(vtok[:, c], ps[6 + c][:, :].rearrange("p (a d) -> p a d", a=GV))
                last.then_inc(vtok_taken, 1)
                for c in range(2):
                    act.wait_ge(arg_ready, 2 * g + c + 1)
                    if c == 1:
                        A(Eg, ps[5][:, :].rearrange("p (a t) -> p a t", a=GV), ACT.Exp)
                    A(Dc[:, c], Dc[:, c], ACT.Exp)
                    act.drain()
                    act.sem_inc(dexp_ready, 1)
                act.wait_ge(bank_ready[2], 2 * g + 2)
                A(zs[:, 2:4], ps[2][:, :].rearrange("p (h t) -> p h t", h=2), ACT.Silu).then_inc(bank_taken[2], 1)
                act.wait_ge(apply_pe, 6 * g + 2)
                nc.scalar.copy(Sst, ps[4][:, :].rearrange("p (a d) -> p a d", a=GV)).then_inc(apply_act, 1)
                act.wait_ge(apply_pe, 6 * g + 3)
                nc.scalar.copy(oT[:, ds(GV * g, GV), 0:P], ps[7][:, :].rearrange("p (a t) -> p a t", a=GV)).then_inc(apply_act, 1)
                act.wait_ge(apply_pe, 6 * g + 6)
                nc.scalar.copy(oT[:, ds(GV * g, GV), P:T], ps[6][:, :].rearrange("p (a t) -> p a t", a=GV)).then_inc(apply_act, 1)
                act.drain()
                A(sq.rearrange("p (a t) -> p a t", a=GV), oT[:, ds(GV * g, GV), :], ACT.Square).then_inc(osq_ready, 1)
                act.wait_ge(oss_ready, g + 1)
                for i in range(2):
                    A(rn[:, i * 512:i * 512 + 512], ps[3 + i][:, :], ACT.Ln, scale=1.0 / P, bias=eps_l2)
                act.drain()
                A(rn, rn, ACT.Exp, scale=-0.5).then_inc(orn_ready, 1)
            act.sem_inc(phase_done[0], 1)
            act.wait_ge(phase_done[0], 4)

            def take_u(bank, use, k):
                act.wait_ge(bank_ready[bank], use + 1)
                nc.scalar.copy(uT[:, k, :], ps[bank][:, :].rearrange("p (k t) -> p k t", k=2)).then_inc(bank_taken[bank], 1)

            with act.Fori(0, 2) as q:
                for r in range(3):
                    take_u(r, U_USE + q, ds(6 * q + 2 * r, 2))
            for r in range(6, 8):
                take_u(r % 3, U_USE + 2, slice(2 * r, 2 * r + 2))
            act.wait_ge(s5_dve, 1)
            A(coef[:, 2], coef[:, 2], ACT.Exp)
            act.drain()
            act.sem_inc(s5_act, 1)
            act.wait_ge(s5_dve, 2)
            A(coef[:, 3], coef[:, 3], ACT.Exp)
            A(coef[:, 4], coef[:, 4], ACT.Sin)
            A(coef[:, 5], coef[:, 5], ACT.Sin)
            act.drain()
            act.sem_inc(s5_act, 1)
            for n in range(0, 16):
                act.wait_ge(s5_tr, n + 2)
                dst = (BT if n < 8 else CT)[:, (n // 4) % 2, 4 * (n % 4):4 * (n % 4) + 4, :]
                src = ps[4 + n % 4][:, :].rearrange("p (k m) -> p k m", k=4)
                if n >= 12:
                    A(dst, src, ACT.Copy, scale=-1.0).then_inc(s5_trc, 1)
                else:
                    nc.scalar.copy(dst, src).then_inc(s5_trc, 1)
            act.sem_inc(bu_taken, 1)
            view = SS[:, 1:STEPS + 1].rearrange("p t c (h k i) -> p h c i k t", h=2, i=4)
            with act.Fori(0, NCH) as ch:
                for c in range(2):
                    for kh in range(2):
                        act.wait_ge(bu_ready, 4 * ch + 2 * c + kh + 1)
                        for i in range(4):
                            nc.scalar.copy(view[:, kh, c, i], ps[4 + i][:, :].rearrange("p (k t) -> p k t", k=8))
                        act.drain()
                        act.sem_inc(bu_taken, 1)
                act.sem_inc(chunk_filled, 1)
                for h in range(2):
                    act.wait_ge(bank_ready[0], DN_USE + 1 + 2 * ch + h)
                    act.wait_ge(merged_ready, 2 * ch + h + 1)
                    A(gdt, ps[0][:, :], ACT.Sigmoid)
                    act.drain()
                    act.sem_inc(bank_taken[0], 1)
                    act.sem_inc(gd_ready, 1)
            act.sem_inc(phase_done[1], 1)
            act.wait_ge(y_taken, NCH + 1)
            for i in range(4):
                last = A(uT[:, 4 * i:4 * i + 4], uT[:, 4 * i:4 * i + 4], ACT.Gelu_apprx_tanh)
            act.drain()
            act.sem_inc(gelu_done, 1)
            with act.Fori(0, 8) as c:
                act.wait_ge(glu_used, c + 1)
                act.wait_ge(bank_ready[1], GLU_USE + c + 1)
                A(ta, ps[1][:, :], ACT.Sigmoid).then_inc(bank_taken[1], 1)
                act.wait_ge(bank_ready[2], GS5_USE + 1 + c)
                A(tb, ps[2][:, :], ACT.Sigmoid).then_inc(bank_taken[2], 1)
                act.drain()
                act.sem_inc(glu_ready, 1)
            act.sem_inc(phase_done[2], 1)
            act.sem_inc(phase_done[3], 1)
            for m in range(MT):
                act.wait_ge(ln_step, m + 1)
                v = stats[:, 50:51]
                A(v, v, ACT.Ln, bias=eps_ln)
                act.drain()
                A(v, v, ACT.Exp, scale=-0.5)
                act.drain()
                act.sem_inc(ln_act, 1)
            for i in range(0, 8, 2):
                act.wait_ge(ht_ready, i + 1)
                nc.scalar.copy(h1T[:, 2 * i:2 * i + 2, :], ps[i][:, :].rearrange("p (k t) -> p k t", k=2)).then_inc(ht_taken, 1)
            for r in range(TOP_K):
                act.wait_ge(rexp_in, r + 1)
                A(rm[:, 4 + r], rm[:, 4 + r], ACT.Exp).then_inc(rexp_out, 1)

            def hidden(e):
                act.wait_ge(gate_taken, e + 2)
                A(sg, gb, ACT.Sigmoid, scale=SW_ALPHA).then_inc(sig_ready, 1)

            def turn(e):
                act.wait_ge(htr_ready, e + 1)
                for m in range(MT):
                    last = nc.scalar.copy(hT[:, :, m * P:m * P + P], ps[4 + m][:, :].rearrange("p (k t) -> p k t", k=KF))
                last.then_inc(htr_taken, 1)

            hidden(0)
            with act.Fori(1, N_E) as e:
                hidden(e)
                turn(e - 1)
            turn(N_E - 1)
            for m in range(MT):
                act.wait_ge(ln_step, MT + m + 1)
                v = stats[:, 50:51]
                A(v, v, ACT.Ln, bias=eps_ln)
                act.drain()
                A(v, v, ACT.Exp, scale=-0.5)
                act.drain()
                act.sem_inc(ln_act, 1)

        @block.vector
        def _(dve):
            V = nc.vector
            for b in range(3):
                dve.sem_inc(bank_taken[b], 1)
            dve.sem_inc(conv_taken, 2)
            for i in range(1, 8, 2):
                dve.wait_ge(xt_ready, i + 1)
                V.tensor_copy(xT[:, 2 * i:2 * i + 2, :], ps[i][:, :].rearrange("p (k t) -> p k t", k=2)).then_inc(xt_taken, 1)
            dve.wait_ge(bd_ready, 1)
            bd = ps[0][:, 0:128].rearrange("p (m c) -> p m c", m=2)
            V.tensor_tensor(sp0[:, 1], bd[:, :, 32:64], dtrow.unsqueeze(1).to_broadcast([P, 2, 32]), ALU.add)
            dve.drain()
            V.scalar_tensor_tensor(out=sp0[:, 0], in0=sp0[:, 1], scalar=-1.0, in1=sp0[:, 1], op0=ALU.mult, op1=ALU.min)
            dve.drain()
            dve.sem_inc(sp_in, 1)
            dve.wait_ge(sp_done, 1)
            V.scalar_tensor_tensor(out=sp0[:, 1], in0=sp0[:, 1], scalar=0.0, in1=sp0[:, 0], op0=ALU.max, op1=ALU.add)
            dve.drain()
            V.scalar_tensor_tensor(out=glog, in0=sp0[:, 1], scalar=-1.0,
                                   in1=arow.unsqueeze(1).to_broadcast([P, 2, 32]), op0=ALU.mult, op1=ALU.mult)
            dve.drain()
            dve.sem_inc(glog_ready, 1)
            dve.wait_ge(gcum_ready, 1)
            V.tensor_copy(gcum, ps[0][:, 0:64].rearrange("p (m c) -> p m c", m=2))
            dve.drain()
            V.tensor_tensor(kd, ps[0][:, 64:96], gcum[:, 0], ALU.subtract)
            dve.drain()
            dve.sem_inc(kd_in, 1)
            dve.wait_ge(kd_out, 1)
            V.tensor_scalar(neg_eg, neg_eg, -1.0, None, ALU.mult)
            dve.drain()
            dve.sem_inc(prologue_done, 1)

            with dve.Fori(0, GROUPS) as g:
                for r, tile in enumerate((GQ * g, H_QK + GQ * g, 2 * H_QK + GV * g, 2 * H_QK + 2 + GV * g)):
                    dve.wait_ge(bank_ready[r % 3], 2 * g + r // 3 + 1)
                    dve.wait_ge(conv_taken, 4 * g + r + 1)
                    for ct in range(2):
                        V.tensor_scalar(cv[:, r % 2, ct * T:ct * T + T], ps[r % 3][:, ct * T:ct * T + T],
                                        cw[:, ds(tile + ct, 1), 3:4].rearrange("p a b -> p (a b)"), None, ALU.mult)
                    dve.drain()
                    for sh in range(1, 4):
                        for ct in range(2):
                            dst = cv[:, r % 2, ct * T + sh:ct * T + T]
                            V.scalar_tensor_tensor(out=dst, in0=ps[r % 3][:, ct * T:ct * T + T - sh],
                                                   scalar=cw[:, ds(tile + ct, 1), 3 - sh:4 - sh].rearrange("p a b -> p (a b)"),
                                                   in1=dst, op0=ALU.mult, op1=ALU.add)
                        dve.drain()
                    dve.sem_inc(bank_taken[r % 3], 1)
                    dve.sem_inc(conv_ready, 1)
                dve.wait_ge(rn_ready, g + 1)
                V.tensor_tensor(qkT.rearrange("p i h t -> p (i h t)"), qkT.rearrange("p i h t -> p (i h t)"), rn,
                                ALU.mult).then_inc(qk_ready, 1)
                dve.wait_ge(tok_ready, g + 1)
                V.tensor_copy(ktok, ps[5][:, 0:GQ * P].rearrange("p (b d) -> p b d", b=GQ)).then_inc(tok_taken, 1)
                for c in range(2):
                    dve.wait_ge(gb_ready, 2 * g + c + 1)
                    for a in range(GV):
                        V.tensor_scalar(Dc[:, c, a], ps[3 + 2 * c][:, a * P:a * P + P],
                                        gcum[:, c, ds(GV * g + a, 1)], 0.0, ALU.subtract, ALU.min)
                    dve.drain()
                    dve.sem_inc(arg_ready, 1)
                for c in range(2):
                    dve.wait_ge(kq_ready, 2 * g + c + 1)
                    dve.wait_ge(dm_ready, 2 * g + c + 1)
                    for a in range(GV):
                        V.scalar_tensor_tensor(out=At[:, c, a], in0=ps[4 + 2 * c][:, (a // 2) * P:(a // 2) * P + P],
                                               scalar=beta[:, c, ds(GV * g + a, 1)], in1=Dc[:, c, a],
                                               op0=ALU.mult, op1=ALU.mult)
                    V.tensor_tensor(attn[:, c].rearrange("p (b r) t -> p b r t", r=2),
                                    ps[4 + 2 * c][:, 2 * P:4 * P].rearrange("p (b t) -> p b t", b=2).unsqueeze(2)
                                    .to_broadcast([P, GQ, 2, P]),
                                    Dm[:, c].rearrange("p (b r) t -> p b r t", r=2), ALU.mult)
                    dve.drain()
                    dve.sem_inc(t_ready[c], 1)
                with dve.Fori(0, LEVELS) as lv:
                    for c in range(2):
                        dve.wait_ge(p_ready[c], 7 * g + lv + 1)
                        V.tensor_tensor(Pm[:, c], ps[3 + 2 * c][:, :].rearrange("p (a t) -> p a t", a=GV),
                                        level_mask[:, ds(lv, 1), :].to_broadcast([P, GV, P]), ALU.mult).then_inc(pm_ready[c], 1)
                    for c in range(2):
                        dve.wait_ge(x_ready[c], 7 * g + lv + 1)
                        V.tensor_tensor(Ti[:, c], Ti[:, c], ps[3 + 2 * c][:, :].rearrange("p (a t) -> p a t", a=GV),
                                        ALU.subtract)
                        V.tensor_tensor(Tt[:, c], Tt[:, c], ps[4 + 2 * c][:, :].rearrange("p (a t) -> p a t", a=GV),
                                        ALU.subtract)
                        dve.drain()
                        dve.sem_inc(t_ready[c], 1)

                def by_head(v, width):
                    return v.unsqueeze(2).to_broadcast([P, GV, width])

                dve.wait_ge(apply_pe, 6 * g + 1)
                V.tensor_tensor(vn[:, 0], ps[3][:, :].rearrange("p (a d) -> p a d", a=GV),
                                by_head(beta[:, 0, ds(GV * g, GV)], P), ALU.mult).then_inc(apply_dve, 1)
                dve.wait_ge(apply_pe, 6 * g + 4)
                V.tensor_tensor(R, ps[5][:, :].rearrange("p (a d) -> p a d", a=GV),
                                by_head(neg_eg[:, ds(GV * g, GV)], P), ALU.mult)
                dve.drain()
                V.tensor_tensor(R, R, vtok[:, 1], ALU.add).then_inc(apply_dve, 1)
                dve.wait_ge(apply_pe, 6 * g + 5)
                V.tensor_tensor(vn[:, 1], ps[3][:, :].rearrange("p (a d) -> p a d", a=GV),
                                by_head(beta[:, 1, ds(GV * g, GV)], P), ALU.mult).then_inc(apply_dve, 1)
                dve.wait_ge(orn_ready, g + 1)
                og = oT[:, ds(GV * g, GV), :]
                V.tensor_tensor(og, og, rn.rearrange("p (a t) -> p a t", a=GV), ALU.mult)
                dve.drain()
                dve.wait_ge(bank_taken[2], 2 * g + 3)
                V.scalar_tensor_tensor(out=og, in0=og, scalar=normw, in1=zs, op0=ALU.mult, op1=ALU.mult)
                dve.drain()
                dve.sem_inc(o_ready, 1)
                dve.sem_inc(prologue_done, 1)
            dve.sem_inc(phase_done[0], 1)
            dve.wait_ge(phase_done[0], 4)

            dve.wait_ge(s5_loaded, 160)
            V.tensor_copy(spar[0:NJ, 2, :].rearrange("p (g n) -> p g n", g=2),
                          coef[0:NJ, 15, 0:2].unsqueeze(2).to_broadcast([NJ, 2, 64]))
            dve.drain()
            dve.sem_inc(s5_step, 1)
            dve.wait_ge(s5_tr, 1)
            LRE, LIM, DT, MAG, SIN, COS, ARE, AIM, NUM, DEN, FRE, FIM, X1, X2 = (coef[:, i] for i in range(14))
            V.tensor_scalar(LRE, ps[3][:, 0:NJ], -1e-4, None, ALU.min)
            V.tensor_copy(LIM, ps[3][:, NJ:2 * NJ])
            V.tensor_copy(DT, ps[3][:, 2 * NJ:3 * NJ])
            dve.drain()
            dve.sem_inc(s5_dve, 1)
            dve.wait_ge(s5_act, 1)

            V.tensor_tensor(MAG, LRE, DT, ALU.mult)
            V.tensor_tensor(X1, LIM, DT, ALU.mult)
            dve.drain()
            V.tensor_scalar(itmp[:, :], X1, 1.0 / TWO_PI, None, ALU.mult)
            dve.drain()
            V.tensor_copy(X2, itmp[:, :])
            dve.drain()
            V.scalar_tensor_tensor(out=X1, in0=X2, scalar=-TWO_PI_HI, in1=X1, op0=ALU.mult, op1=ALU.add)
            dve.drain()
            V.scalar_tensor_tensor(out=X1, in0=X2, scalar=-TWO_PI_LO, in1=X1, op0=ALU.mult, op1=ALU.add)
            dve.drain()
            V.tensor_scalar(SIN, X1, PI_SAFE, -PI_SAFE, ALU.min, ALU.max)
            V.tensor_scalar(X1, X1, math.pi / 2, None, ALU.add)
            dve.drain()
            V.tensor_scalar(X2, X1, math.pi, -TWO_PI, ALU.is_gt, ALU.mult)
            dve.drain()
            V.tensor_tensor(X1, X1, X2, ALU.add)
            dve.drain()
            V.tensor_scalar(COS, X1, PI_SAFE, -PI_SAFE, ALU.min, ALU.max)
            dve.drain()
            dve.sem_inc(s5_dve, 1)
            dve.wait_ge(s5_act, 2)
            V.tensor_tensor(ARE, MAG, COS, ALU.mult)
            V.tensor_tensor(AIM, MAG, SIN, ALU.mult)
            V.tensor_tensor(X1, LRE, LRE, ALU.mult)
            V.tensor_tensor(X2, LIM, LIM, ALU.mult)
            dve.drain()
            V.tensor_tensor(DEN, X1, X2, ALU.add)
            V.tensor_copy(Arr, ARE.unsqueeze(1).to_broadcast([P, 2, NJ]))
            V.tensor_copy(Aim[:, 1], AIM)
            V.tensor_scalar(Aim[:, 0], AIM, -1.0, None, ALU.mult)
            dve.drain()
            V.reciprocal(X2, DEN)
            V.tensor_scalar(NUM, ARE, -1.0, None, ALU.add)
            dve.drain()
            V.tensor_tensor(FRE, NUM, LRE, ALU.mult)
            V.tensor_tensor(X1, AIM, LIM, ALU.mult)
            dve.drain()
            V.tensor_tensor(FRE, FRE, X1, ALU.add)
            V.tensor_tensor(FIM, AIM, LRE, ALU.mult)
            V.tensor_tensor(DEN, NUM, LIM, ALU.mult)
            dve.drain()
            V.tensor_tensor(FIM, FIM, DEN, ALU.subtract)
            V.tensor_tensor(FRE, FRE, X2, ALU.mult)
            dve.drain()
            V.tensor_tensor(FIM, FIM, X2, ALU.mult)
            V.memset(bwide, 0.0)
            dve.drain()
            fr = FRE.unsqueeze(2).to_broadcast([P, NJ, 16])
            fi = FIM.unsqueeze(2).to_broadcast([P, NJ, 16])
            for c, (p1, p2, op) in enumerate(((0, 1, ALU.subtract), (1, 0, ALU.add))):
                V.tensor_tensor(bb[:, c], braw[:, p1], fr, ALU.mult)
                V.tensor_tensor(bt1, braw[:, p2], fi, ALU.mult)
                dve.drain()
                for g2 in range(2):
                    h = slice(64 * g2, 64 * g2 + 64)
                    V.tensor_tensor(bwide[h, c, :, 16 * g2:16 * g2 + 16], bb[h, c], bt1[h], op)
                dve.drain()
            dve.sem_inc(s5_step, 1)
            for c in range(2):
                for g2 in range(2):
                    V.tensor_scalar(cwide[:, c, :, g2, :], craw[:, c], halfmask[:, g2:g2 + 1], None, ALU.mult)
            dve.drain()
            dve.sem_inc(s5_step, 1)
            dve.wait_ge(s5_trc, 16)
            dve.sem_inc(s5_step, 1)
            dve.sem_inc(y_taken, 1)
            dve.sem_inc(merged_ready, 1)

            with dve.Fori(0, NCH) as ch:
                V.tensor_copy(uch, uT[:, :, ds(STEPS * ch, STEPS)]).then_inc(uch_ready, 1)
                for h in range(2):
                    dve.wait_ge(bank_ready[1], DN_USE + 1 + 2 * ch + h)
                    dve.wait_ge(gd_ready, 2 * ch + h + 1)
                    V.tensor_tensor(mg[:, ds(4 * ch + 2 * h, 2), :], ps[1][:, :].rearrange("p (k t) -> p k t", k=2),
                                    gdt.rearrange("p (k t) -> p k t", k=2), ALU.mult)
                    dve.drain()
                    dve.sem_inc(bank_taken[1], 1)
                    dve.sem_inc(merged_ready, 1)
                dve.wait_ge(y_ready, ch + 1)
                for kh in range(2):
                    uv = uT[:, kh * 8:kh * 8 + 8, ds(STEPS * ch, STEPS)]
                    V.tensor_tensor(ytmp, uv, dsk[:, kh * 8:kh * 8 + 8].unsqueeze(2).to_broadcast([P, 8, STEPS]), ALU.mult)
                    dve.drain()
                    V.tensor_tensor(uv, ytmp, ps[2 + kh][:, :].rearrange("p (k t) -> p k t", k=8), ALU.add)
                    dve.drain()
                dve.sem_inc(y_taken, 1)
            dve.sem_inc(phase_done[1], 1)
            dve.wait_ge(phase_done[1], 4)
            dve.sem_inc(glu_used, 1)
            with dve.Fori(0, 8) as c:
                dve.wait_ge(glu_ready, c + 1)
                dve.wait_ge(bank_ready[0], GLU_USE + c + 1)
                V.tensor_tensor(ta, ta, ps[0][:, :], ALU.mult)
                dve.drain()
                dve.sem_inc(bank_taken[0], 1)
                V.tensor_tensor(ta, ta, tb, ALU.mult)
                dve.drain()
                mv = mg[:, ds(2 * c, 2), :]
                V.tensor_tensor(mv, mv, ta.rearrange("p (k t) -> p k t", k=2), ALU.add)
                dve.drain()
                dve.sem_inc(glu_used, 1)
            dve.sem_inc(phase_done[2], 1)

            dve.wait_ge(x_loaded, 16)

            def take_mix(r, use, cols):
                dve.wait_ge(bank_ready[r % 3], use)
                hv = h1[:, :, cols]
                V.scalar_tensor_tensor(out=hv, in0=hv, scalar=ALPHA, in1=ps[3 + r % 3][:, :].rearrange("p (m n) -> p m n", m=2),
                                       op0=ALU.mult, op1=ALU.add)
                dve.drain()
                dve.sem_inc(bank_taken[r % 3], 1)

            for r in range(2):
                take_mix(r, MIX_USE[r] + 1, slice(SC * r, SC * r + SC))
            with dve.Fori(0, 2) as q:
                for r in range(2, 5):
                    take_mix(r, MIX_USE[r % 3] + r // 3 + 1 + q, ds(768 * q + SC * r, SC))
            dve.wait_ge(ln_loaded, 32)

            def norm(m, rows, n):
                for i in range(4):
                    V.bn_stats(stats[:, 6 * i:6 * i + 6], h1[:, m, 512 * i:512 * i + 512])
                dve.drain()
                V.bn_aggr(stats[:, 49:51], stats[:, 0:24])
                dve.drain()
                dve.sem_inc(ln_step, 1)
                dve.wait_ge(ln_act, n + 1)
                V.tensor_scalar(h1[:, m], h1[:, m], stats[:, 49:50], stats[:, 50:51], ALU.subtract, ALU.mult)
                dve.drain()
                V.tensor_tensor(h1[:, m], h1[:, m], rows[:, 0], ALU.mult)
                dve.drain()
                V.tensor_tensor(h1[:, m], h1[:, m], rows[:, 1], ALU.add)
                dve.drain()

            for m in range(MT):
                norm(m, lnrow, m)
            dve.sem_inc(h1_ready, 1)
            dve.sem_inc(phase_done[3], 1)
            for i in range(1, 8, 2):
                dve.wait_ge(ht_ready, i + 1)
                V.tensor_copy(h1T[:, 2 * i:2 * i + 2, :], ps[i][:, :].rearrange("p (k t) -> p k t", k=2)).then_inc(ht_taken, 1)

            lg, eq, oh, rev = rt[:, 1], rt[:, 2], rt[:, 3], rt[:, 4]
            dve.wait_ge(rt_loaded, 64)
            dve.wait_ge(logit_ready, 1)
            V.tensor_tensor(lg, ps[0][:, 0:MT * N_E].rearrange("p (m e) -> p m e", m=MT), rt[:, 7], ALU.add)
            V.memset(wt, 0.0)
            dve.wait_ge(rev_ready, 1)
            dve.drain()

            def wide(v):
                return v.unsqueeze(2).to_broadcast([P, MT, N_E])

            for r in range(TOP_K):
                V.tensor_reduce(rm[:, r], lg, AX_X, ALU.max)
                dve.drain()
                V.tensor_tensor(rm[:, 4 + r], rm[:, r], rm[:, 0], ALU.subtract)
                V.tensor_tensor(eq, lg, wide(rm[:, r]), ALU.is_equal)
                dve.drain()
                dve.sem_inc(rexp_in, 1)
                V.tensor_tensor(eq, eq, rev, ALU.mult)
                dve.drain()
                V.tensor_reduce(rt[:, 5, :, 0:1].rearrange("p m o -> p (m o)"), eq, AX_X, ALU.max)
                dve.drain()
                V.tensor_tensor(oh, eq, rt[:, 5, :, 0:1].to_broadcast([P, MT, N_E]), ALU.is_equal)
                dve.drain()
                V.scalar_tensor_tensor(out=lg, in0=oh, scalar=-3.0e38, in1=lg, op0=ALU.mult, op1=ALU.add)
                dve.wait_ge(rexp_out, r + 1)
                V.tensor_tensor(oh, oh, wide(rm[:, 4 + r]), ALU.mult)
                dve.drain()
                V.tensor_tensor(wt, wt, oh, ALU.add)
                dve.drain()
            V.tensor_reduce(rm[:, 0], wt, AX_X, ALU.add)
            dve.drain()
            V.reciprocal(rm[:, 1], rm[:, 0])
            dve.drain()
            V.tensor_tensor(wt, wt, wide(rm[:, 1]), ALU.mult)
            dve.drain()
            dve.sem_inc(wt_ready, 1)
            dve.wait_ge(wtt_ready, 1)
            V.tensor_copy(wtT[:, :], ps[1][0:N_E, 0:T]).then_inc(wtt_taken, 1)
            dve.wait_ge(bd2_ready, 1)
            for m in range(MT):
                for n in range(4):
                    V.tensor_copy(acc[:, m, n * 512:n * 512 + 512], ps[(2 + 4 * m + n) % 8][:, :])
            dve.drain()
            dve.sem_inc(acc0_ready, 1)
            dve.sem_inc(gate_taken, 1)
            for b in range(2):
                dve.sem_inc(dn_taken[b], 1)

            def take_gate(e):
                dve.wait_ge(gate_done, e + 1)
                dve.wait_ge(brow_loaded, 32 * e + 32)
                for m in range(MT):
                    V.tensor_tensor(gb[:, m], ps[m][:, :], brow[:, 0], ALU.add)
                dve.drain()
                V.tensor_scalar(gb, gb, LIMIT, None, ALU.min)
                dve.drain()
                dve.sem_inc(gate_taken, 1)

            def take_up(e):
                dve.wait_ge(up_done, e + 1)
                for m in range(MT):
                    V.tensor_tensor(hb[:, m], ps[2 + m][:, :], brow[:, 1], ALU.add)
                dve.drain()
                dve.sem_inc(up_taken, 2)
                V.tensor_scalar(hb, hb, LIMIT, -LIMIT, ALU.min, ALU.max)
                dve.drain()
                V.scalar_tensor_tensor(out=hb, in0=hb, scalar=1.0, in1=gb, op0=ALU.add, op1=ALU.mult)
                dve.drain()
                dve.wait_ge(sig_ready, e + 1)
                for m in range(MT):
                    wcol = wt[:, m, ds(e, 1)] if not isinstance(e, int) else wt[:, m, e:e + 1]
                    V.scalar_tensor_tensor(out=hb[:, m], in0=hb[:, m], scalar=wcol, in1=sg[:, m],
                                           op0=ALU.mult, op1=ALU.mult)
                dve.drain()
                dve.sem_inc(hb_ready, 1)

            def add_down(e):
                for n in range(8):
                    av = acc[:, n // 4, (n % 4) * 512:(n % 4) * 512 + 512]
                    dve.wait_ge(dn_ready[n % 2], 4 * e + n // 2 + 1)
                    V.tensor_tensor(av, av, ps[6 + n % 2][:, :], ALU.add).then_inc(dn_taken[n % 2], 1)

            take_gate(0)
            take_up(0)
            with dve.Fori(1, N_E) as e:
                take_gate(e)
                add_down(e - 1)
                take_up(e)
            add_down(N_E - 1)
            dve.wait_ge(ln2_loaded, 32)
            dve.drain()
            for m in range(MT):
                V.scalar_tensor_tensor(out=h1[:, m], in0=h1[:, m], scalar=ALPHA, in1=acc[:, m], op0=ALU.mult, op1=ALU.add)
                dve.drain()
                norm(m, ln2row, MT + m)
                dve.sem_inc(out_ready, 1)


_INS = ['x', 'w_in', 'dn_conv_w', 'dn_a_log', 'dn_dt_bias', 'dn_norm_w', 'w_dn_out', 's5_lam_re', 's5_lam_im',
        's5_log_dt', 's5_b_re', 's5_b_im', 's5_c_re', 's5_c_im', 's5_d', 'w_glu_a', 'w_glu_b', 'w_mix_out',
        'ln1_g', 'ln1_b', 'w_router', 'b_router', 'w_gate', 'b_gate', 'w_up', 'b_up', 'w_down', 'b_down',
        'ln2_g', 'ln2_b']


def kernel(**inputs):
    import numpy as _np
    import concourse.bacc as _bacc
    from concourse import mybir as _mybir
    from concourse.bass_utils import run_bass_kernel_spmd as _run

    nc = _bacc.Bacc("TRN2", target_bir_lowering=False, num_devices=1)
    arrays, args = {}, []
    for name in _INS:
        a = _np.ascontiguousarray(inputs[name])
        arrays[f"in_{name}_dram"] = a
        ap = nc.dram_tensor(f"in_{name}_dram", a.shape, _mybir.dt.from_np(a.dtype), kind="ExternalInput").ap()
        args.append(ap if name == 'x' else ap[0])
    o = nc.dram_tensor("out_0_dram", (1, T, D), F32, kind="ExternalOutput").ap()
    build(nc, *args, o)
    r = _run(nc, [arrays], core_ids=[0])
    return r.results[0]["out_0_dram"]
```

```python
import math
from contextlib import ExitStack

import concourse.bass as bass
from concourse import mybir

ALU = mybir.AluOpType
ACT = mybir.ActivationFunctionType
F32 = mybir.dt.float32
I32 = mybir.dt.int32
AX_X = mybir.AxisListType.X

P = 128
T = 256
MT = T // P
D = 2048
KD = D // P
SC = 256
RING = 3
H_V, H_QK = 32, 16
GROUPS = 8
GV, GQ = H_V // GROUPS, H_QK // GROUPS
LEVELS = 7
OFF_Q = 2048
OFF_K = OFF_Q + H_QK * P
OFF_V = OFF_K + H_QK * P
OFF_Z = OFF_V + H_V * P
OFF_BD = OFF_Z + H_V * P
OFF_GS5 = OFF_BD + 2 * H_V
OFF_GDN = OFF_GS5 + D
STEPS = 64
NCH = T // STEPS
NJ = 64
N_E, TOP_K, F_E = 32, 4, 512
KF = F_E // P
ALPHA = 2.0 ** 0.25
CAP = 64
LIMIT, SW_ALPHA = 7.0, 1.702
LN_EPS, RMS_EPS, L2_EPS = 1e-5, 1e-6, 1e-6
TWO_PI = 2.0 * math.pi
TWO_PI_HI = 6.28125
TWO_PI_LO = TWO_PI - TWO_PI_HI
PI_SAFE = 3.1415925

S_GROUP = 0
S_U = S_GROUP + 6 * GROUPS
S_DN = S_U + 8
S_GLU = S_DN + 24
S_MIX = S_GLU + 24
U_USE = 2 * GROUPS
DN_USE = U_USE + 3
GLU_USE = DN_USE + 8
GS5_USE = U_USE + 2
MIX_USE = (GLU_USE + 8, GLU_USE + 8, GS5_USE + 8)


def build(nc, x, w_in, conv_w, a_log, dt_bias, norm_w, w_dn, lam_re, lam_im, log_dt, b_re, b_im, c_re, c_im,
          d_skip, w_glu_a, w_glu_b, w_mix, ln1_g, ln1_b, w_router, b_router, w_gate, b_gate, w_up, b_up,
          w_down, b_down, ln2_g, ln2_b, out):
    ds = bass.ds
    with ExitStack() as ctx:
        def sb(name, shape, dt=F32):
            return ctx.enter_context(nc.sbuf_tensor(name, shape, dt))

        def sem(name):
            return ctx.enter_context(nc.semaphore(name))

        ps = [ctx.enter_context(nc.psum_tensor(f"bank{i}", [P, 512], F32)) for i in range(8)]
        ident = sb("ident", [P, P])
        masks = sb("masks", [P, 8 * P])
        upper = masks[:, 0:P]
        ones = sb("ones", [P, P])
        level_mask = masks[:, P:8 * P].rearrange("p (l t) -> p l t", l=LEVELS)
        uch = masks[:, :].rearrange("p (k t) -> p k t", k=KD)
        cw = sb("cw", [P, 64, 4])
        small = sb("small", [P, 448])
        beta = small[:, 0:64].rearrange("p (c h) -> p c h", c=2)
        gcum = small[:, 64:128].rearrange("p (c h) -> p c h", c=2)
        glog = small[:, 128:192].rearrange("p (c h) -> p c h", c=2)
        neg_eg = small[:, 192:224]
        kd = small[:, 224:256]
        arow = small[:, 256:288]
        dtrow = small[:, 288:320]
        normw = small[:, 320:321]
        dsk = small[:, 321:337]
        stats = small[:, 340:396]
        eps_ln = small[:, 396:397]
        eps_l2 = small[:, 397:398]
        lnq = small[:, 398:399]
        zero1 = small[:, 399:400]
        halfmask = small[:, 400:402]
        ggrp = small[:, 402:410].rearrange("p (c a) -> p c a", c=2)
        itmp = sb("itmp", [P, NJ], I32)

        ARENA = 51000
        arena = sb("arena", [P, ARENA])

        def at(off, *dims):
            n = 1
            for d in dims:
                n *= d
            assert off + n <= ARENA, (off, dims)
            v = arena[:, off:off + n]
            if len(dims) == 1:
                return v
            names = "abcde"[:len(dims)]
            return v.rearrange(f"p ({' '.join(names)}) -> p {' '.join(names)}",
                               **{names[i]: dims[i] for i in range(1, len(dims))})

        ring = at(0, RING, KD, SC)
        XT = 12288
        xT = at(XT, KD, T)
        OT = 16384
        oT = at(OT, H_V, T)
        SH = 24576
        xtok = at(SH, MT, D)
        wbd = at(SH + 4096, KD, 2 * H_V)
        sp0 = at(SH + 5120, 2, 2, 32)
        qkT = at(SH, 2, GQ, T)
        ktok = at(SH + 1024, GQ, P)
        vtok = at(SH + 1280, 2, GV, P)
        cv = at(SH + 2304, 2, 512)
        sq = at(SH + 3328, 1024)
        rn = at(SH + 4352, 1024)
        Eg = at(SH + 5376, GV, P)
        kdec = at(SH + 5888, GV, P)
        vn = at(SH + 6400, 2, GV, P)
        Sst = at(SH + 7424, GV, P)
        R = at(SH + 7936, GV, P)
        qd = at(SH + 8448, GV, P)
        zs = at(SH + 8960, GV, T)
        w0 = SH + 9984
        gU = at(w0, 2, GV, P)
        Dc = at(w0 + 1024, 2, GV, P)
        Dm = at(w0 + 2048, 2, GV, P)
        At = at(w0 + 3072, 2, GV, P)
        attn = at(w0 + 4096, 2, GV, P)
        Ti = at(w0 + 5120, 2, GV, P)
        Tt = at(w0 + 6144, 2, GV, P)
        Pm = at(w0 + 7168, 2, GV, P)
        zvT = at(w0 + 8192, GV, T)
        uT = at(SH, KD, T)
        SS0 = SH + 4096
        SS = at(SS0, STEPS + 1, 2, NJ)
        BT0 = SS0 + (STEPS + 1) * 2 * NJ
        BT = at(BT0, 2, KD, P)
        CT = at(BT0 + 4096, 2, KD, P)
        MG = BT0 + 8192
        mg = at(MG, KD, T)
        TM = MG + 4096
        Arr = at(TM, 2, NJ)
        Aim = at(TM + 128, 2, NJ)
        m1 = at(TM + 256, 2, NJ)
        m2 = at(TM + 384, 2, NJ)
        gdt = at(TM + 512, 512)
        ytmp = at(TM + 1024, 8, STEPS)
        spar = at(MG, 3, P)
        coef = at(MG + 384, 16, NJ)
        braw = at(SS0 + 128, 2, NJ, 16)
        bb = at(SS0 + 128 + 2048, 2, NJ, 16)
        bt1 = at(SS0 + 128 + 4096, NJ, 16)
        craw = at(MG + 2048, 2, KD, 64)
        bwide = at(BT0 + 4096, 2, NJ, 32)
        cwide = at(SS0 + 128, 2, KD, 2, 64)
        ta = at(TM + 512, 512)
        tb = at(TM + 1024, 512)
        h1 = at(SH, MT, D)
        acc = at(SH + 4096, MT, D)
        lnrow = at(XT, 2, D)
        h1T = at(XT, KD, T)
        GW = at(SH + 8192, KD, F_E)
        UW = at(SH + 16384, KD, F_E)
        DW = at(OT, KF, D)
        bdn = at(0, D)
        gb = at(2048, MT, F_E)
        sg = at(3072, MT, F_E)
        hb = at(4096, MT, F_E)
        hT = at(5120, KF, T)
        brow = at(6144, 2, F_E)
        wr = at(7168, KD, N_E)
        ln2row = at(8192, 2, D)
        rt = at(TM, 8, MT, N_E)
        wt = rt[:, 0]
        rm = sb("rm", [P, 8, MT])
        wtT = at(TM + 512, T)[0:N_E]

        xg = at(2048, KD, CAP)
        sgb = at(3072, F_E)
        ssg = at(3584, F_E)
        shb = at(4096, F_E)
        shT = at(4608, KF, CAP)
        pwT = at(4864, T)
        ysb = at(0, D)
        Psel = at(TM + 768, MT, CAP)
        Pw = at(TM + 768 + MT * CAP, MT, CAP)
        slots1 = at(TM + 768 + 2 * MT * CAP, CAP)
        flag = sb("flag", [P, 1], I32)

        const_ready = sem("const_ready")
        turn_begun = sem("turn_begun")
        load_free, scan_begun = sem("load_free"), sem("scan_begun")
        pro_loaded = sem("pro_loaded")
        slot_loaded = [sem(f"slot{i}_loaded") for i in range(RING)]
        bank_ready = [sem(f"bank{i}_ready") for i in range(3)]
        bank_taken = [sem(f"bank{i}_taken") for i in range(3)]
        xt_ready, xt_taken = sem("xt_ready"), sem("xt_taken")
        bd_ready, glog_ready, gcum_ready, prologue_done = (sem("bd_ready"), sem("glog_ready"), sem("gcum_ready"),
                                                           sem("prologue_done"))
        sp_in, sp_done, kd_in, kd_out = sem("sp_in"), sem("sp_done"), sem("kd_in"), sem("kd_out")
        s5_dve, s5_act, ln_act, rev_ready = sem("s5_dve"), sem("s5_act"), sem("ln_act"), sem("rev_ready")
        conv_ready, conv_taken = sem("conv_ready"), sem("conv_taken")
        sq_ready, ss_ready, rn_ready, qk_ready = sem("sq_ready"), sem("ss_ready"), sem("rn_ready"), sem("qk_ready")
        tok_ready, tok_taken, vtok_taken = sem("tok_ready"), sem("tok_taken"), sem("vtok_taken")
        gu_ready, gb_ready, arg_ready, dexp_ready, dm_ready = (sem("gu_ready"), sem("gb_ready"), sem("arg_ready"),
                                                              sem("dexp_ready"), sem("dm_ready"))
        kq_ready, aux_ready = sem("kq_ready"), sem("aux_ready")
        t_ready = [sem(f"t{c}_ready") for c in range(2)]
        p_ready = [sem(f"p{c}_ready") for c in range(2)]
        pm_ready = [sem(f"pm{c}_ready") for c in range(2)]
        x_ready = [sem(f"x{c}_ready") for c in range(2)]
        apply_pe, apply_dve, apply_act = sem("apply_pe"), sem("apply_dve"), sem("apply_act")
        osq_ready, oss_ready, orn_ready, o_ready = sem("osq_ready"), sem("oss_ready"), sem("orn_ready"), sem("o_ready")
        z_ready = sem("z_ready")
        phase_done = [sem(f"phase{i}_done") for i in range(5)]
        s5_loaded, s5_tr, s5_trc, s5_step = sem("s5_loaded"), sem("s5_tr"), sem("s5_trc"), sem("s5_step")
        uch_ready = sem("uch_ready")
        bu_ready, bu_taken, chunk_filled, scan_done = (sem("bu_ready"), sem("bu_taken"), sem("chunk_filled"),
                                                       sem("scan_done"))
        y_ready, y_taken, gd_ready, merged_ready = sem("y_ready"), sem("y_taken"), sem("gd_ready"), sem("merged_ready")
        gelu_done = sem("gelu_done")
        glu_ready, glu_used = sem("glu_ready"), sem("glu_used")
        sel_ready, pos_ready, flag_ready, upper_ready = (sem("sel_ready"), sem("pos_ready"), sem("flag_ready"),
                                                         sem("upper_ready"))
        p_built, xg_done, xg_taken, y_copied, sc_done, sc_taken, sdn_done = (
            sem("p_built"), sem("xg_done"), sem("xg_taken"), sem("y_copied"), sem("sc_done"), sem("sc_taken"),
            sem("sdn_done"))
        x_loaded, ln_loaded, ln_step = sem("x_loaded"), sem("ln_loaded"), sem("ln_step")
        h1_ready, ht_ready, ht_taken, logit_ready, wt_ready, wtt_ready, wtt_taken = (
            sem("h1_ready"), sem("ht_ready"), sem("ht_taken"), sem("logit_ready"), sem("wt_ready"),
            sem("wtt_ready"), sem("wtt_taken"))
        rt_loaded, rexp_in, rexp_out = sem("rt_loaded"), sem("rexp_in"), sem("rexp_out")
        bd2_ready, acc0_ready = sem("bd2_ready"), sem("acc0_ready")
        gw_loaded, uw_loaded, dw_loaded, brow_loaded = (sem("gw_loaded"), sem("uw_loaded"), sem("dw_loaded"),
                                                        sem("brow_loaded"))
        gate_done, gate_taken, up_done, up_taken = sem("gate_done"), sem("gate_taken"), sem("up_done"), sem("up_taken")
        sig_ready, hb_ready = sem("sig_ready"), sem("hb_ready")
        htr_ready, htr_taken = sem("htr_ready"), sem("htr_taken")
        dn_ready = [sem(f"down_bank{i}_ready") for i in range(2)]
        dn_taken = [sem(f"down_bank{i}_taken") for i in range(2)]
        ln2_loaded, out_ready, out_done = sem("ln2_loaded"), sem("out_ready"), sem("out_done")

        def in_rows(w):
            return w.rearrange("(p k) n -> p k n", k=KD)

        def tile_rows(w):
            return w.rearrange("(k p) n -> p k n", p=P)

        block = ctx.enter_context(nc.Block())

        @block.sync
        def _(sp):
            sp.dma_start(xtok, x[0].rearrange("(m p) d -> p m d", p=P)).then_inc(pro_loaded, 16)
            sp.dma_start(wbd, in_rows(w_in[:, OFF_BD:OFF_BD + 2 * H_V])).then_inc(pro_loaded, 16)
            sp.dma_start(cw[:, :, :], conv_w.rearrange("(j p) t -> p j t", p=P)).then_inc(pro_loaded, 16)
            sp.dma_start(arow, a_log.partition_broadcast(P)).then_inc(pro_loaded, 16)
            sp.dma_start(dtrow, dt_bias.partition_broadcast(P)).then_inc(pro_loaded, 16)
            sp.dma_start(normw, norm_w.rearrange("(p o) -> p o", o=1)).then_inc(pro_loaded, 16)

            def load_slot(buf, src, bank, taken):
                sp.wait_ge(bank_taken[bank], taken)
                sp.sem_inc(load_free, 1)
                sp.dma_start(ring[:, buf], src).then_inc(slot_loaded[buf], 16)

            with sp.Fori(0, GROUPS) as g:
                for r, col in enumerate((OFF_Q + 256 * g, OFF_K + 256 * g, OFF_V + 512 * g, OFF_V + 256 + 512 * g,
                                         OFF_Z + 512 * g, OFF_Z + 256 + 512 * g)):
                    load_slot(r % RING, in_rows(w_in[:, ds(col, SC)]), r % 3, 2 * g + r // 3 + 1)
            sp.wait_ge(phase_done[0], 4)
            sp.dma_start(spar[0:NJ, 0, :], lam_re.rearrange("(j g) n -> j (g n)", g=2)).then_inc(s5_loaded, 16)
            sp.dma_start(spar[0:NJ, 1, :], lam_im.rearrange("(j g) n -> j (g n)", g=2)).then_inc(s5_loaded, 16)
            sp.dma_start(coef[0:NJ, 15, 0:2], log_dt.rearrange("(j g) -> j g", g=2)).then_inc(s5_loaded, 16)
            for c, b in enumerate((b_re, b_im)):
                bv = b.rearrange("(j g) n q -> g n j q", g=2)
                for g2 in range(2):
                    sp.dma_start(braw[64 * g2:64 * g2 + 64, c], bv[g2]).then_inc(s5_loaded, 16)
            for c, cc in enumerate((c_re, c_im)):
                sp.dma_start(craw[:, c], cc.rearrange("(k a) q n -> (a q) k n", k=KD)).then_inc(s5_loaded, 16)
            sp.dma_start(dsk, d_skip.rearrange("(k a) q -> (a q) k", k=KD), allow_slow_non_contiguous=True).then_inc(s5_loaded, 16)
            with sp.Fori(0, 2) as q:
                for r in range(3):
                    load_slot((S_U + r) % RING, in_rows(w_in[:, ds(768 * q + 256 * r, SC)]), r, U_USE + q + 1)
            for r in range(6, 8):
                load_slot((S_U + r) % RING, in_rows(w_in[:, SC * r:SC * r + SC]), r % 3, U_USE + 3)
            with sp.Fori(0, 8) as c:
                load_slot(S_DN % RING, in_rows(w_in[:, ds(OFF_GDN + SC * c, SC)]), 0, DN_USE + 1 + c)
                for h in range(2):
                    load_slot((S_DN + 1 + h) % RING, tile_rows(w_dn[h * D:h * D + D, ds(SC * c, SC)]), 1,
                              DN_USE + 1 + c)
            with sp.Fori(0, 8) as c:
                load_slot(S_GLU % RING, tile_rows(w_glu_a[:, ds(SC * c, SC)]), 0, GLU_USE + 1 + c)
                load_slot((S_GLU + 1) % RING, tile_rows(w_glu_b[:, ds(SC * c, SC)]), 1, GLU_USE + 1 + c)
                load_slot((S_GLU + 2) % RING, in_rows(w_in[:, ds(OFF_GS5 + SC * c, SC)]), 2, GS5_USE + 1 + c)
            load_slot(S_MIX % RING, tile_rows(w_mix[:, 0:SC]), 0, MIX_USE[0] + 1)
            sp.wait_ge(phase_done[2], 4)
            sp.dma_start(h1, x[0].rearrange("(m p) d -> p m d", p=P)).then_inc(x_loaded, 16)
            sp.dma_start(lnrow[:, 0], ln1_g.partition_broadcast(P)).then_inc(ln_loaded, 16)
            sp.dma_start(lnrow[:, 1], ln1_b.partition_broadcast(P)).then_inc(ln_loaded, 16)
            for r in range(1, 2):
                load_slot((S_MIX + r) % RING, tile_rows(w_mix[:, SC * r:SC * r + SC]), r, MIX_USE[r] + 1)
            with sp.Fori(0, 2) as q:
                for r in range(2, 5):
                    load_slot((S_MIX + r) % RING, tile_rows(w_mix[:, ds(768 * q + SC * r, SC)]), r % 3,
                              MIX_USE[r % 3] + r // 3 + 1 + q)

            def load_gate(e):
                sp.dma_start(GW,
                             w_gate[ds(e, 1)].rearrange("o (k p) n -> p (o k) n", p=P)).then_inc(gw_loaded, 16)

            def load_up(e):
                sp.dma_start(brow[:, 0], b_gate[ds(e, 1)].rearrange("o n -> (o n)").partition_broadcast(P)).then_inc(brow_loaded, 16)
                sp.dma_start(brow[:, 1], b_up[ds(e, 1)].rearrange("o n -> (o n)").partition_broadcast(P)).then_inc(brow_loaded, 16)
                sp.dma_start(UW,
                             w_up[ds(e, 1)].rearrange("o (k p) n -> p (o k) n", p=P)).then_inc(uw_loaded, 16)

            def load_down(e):
                sp.dma_start(DW.rearrange("p k n -> p (k n)"),
                             w_down[ds(e, 1)].rearrange("o (p k) n -> p (o k n)", k=KF)).then_inc(dw_loaded, 16)

            load_gate(0)
            sp.wait_ge(phase_done[3], 4)
            sp.dma_start(wr, w_router.rearrange("(k p) e -> p k e", p=P)).then_inc(rt_loaded, 16)
            sp.dma_start(rt[:, 7, 0], b_router.partition_broadcast(P)).then_inc(rt_loaded, 16)
            sp.dma_start(rt[:, 7, 1], b_router.partition_broadcast(P)).then_inc(rt_loaded, 16)
            sp.dma_start(bdn[0:N_E, :], b_down).then_inc(rt_loaded, 16)
            load_up(0)
            sp.dma_start(ln2row[:, 0], ln2_g.partition_broadcast(P)).then_inc(ln2_loaded, 16)
            sp.dma_start(ln2row[:, 1], ln2_b.partition_broadcast(P)).then_inc(ln2_loaded, 16)
            sp.wait_ge(flag_ready, 1)
            over = sp.value_load(flag[0:1, 0:1], min_val=0, max_val=1)
            with sp.If(over < 1):
                with sp.Fori(0, N_E - 1) as e:
                    sp.wait_ge(gate_done, e + 1)
                    sp.sem_inc(load_free, 1)
                    load_gate(e + 1)
                    sp.wait_ge(y_copied, 4 * e + 2)
                    sp.sem_inc(load_free, 1)
                    load_down(e)
                    sp.wait_ge(up_taken, 2 * e + 2)
                    sp.sem_inc(load_free, 1)
                    load_up(e + 1)
                sp.wait_ge(y_copied, 4 * N_E - 2)
                load_down(N_E - 1)
            with sp.If(over > 0):
                with sp.Fori(0, N_E - 1) as e:
                    sp.wait_ge(gate_done, e + 1)
                    sp.sem_inc(load_free, 1)
                    load_gate(e + 1)
                    sp.wait_ge(dn_taken[1], 4 * e + 1)
                    sp.sem_inc(load_free, 1)
                    load_down(e)
                    sp.wait_ge(up_taken, 2 * e + 2)
                    sp.sem_inc(load_free, 1)
                    load_up(e + 1)
                sp.wait_ge(dn_taken[1], 4 * N_E - 3)
                load_down(N_E - 1)
            for m in range(MT):
                sp.wait_ge(out_ready, m + 1)
                sp.dma_start(out[0, m * P:m * P + P, :], h1[:, m]).then_inc(out_done, 16)
            sp.wait_ge(out_done, 32)

        @block.gpsimd
        def _(pool):
            g = nc.gpsimd
            g.memset(ident[:, :], 0.0)
            g.memset(upper, 1.0)
            g.memset(ones[:, :], 1.0)
            g.memset(level_mask, 0.0)
            g.memset(eps_ln, LN_EPS)
            g.memset(eps_l2, L2_EPS)
            g.memset(zero1, 0.0)
            g.memset(lnq, -0.5 * math.log(P))
            g.memset(halfmask, 1.0)
            pool.drain()
            g.affine_select(out=ident[:, :], in_=ident[:, :], compare_op=ALU.not_equal, fill=1.0, base=0,
                            pattern=[[-1, P]], channel_multiplier=1)
            g.affine_select(out=upper, in_=upper, compare_op=ALU.is_ge, fill=0.0, base=0,
                            pattern=[[1, P]], channel_multiplier=-1)
            for lv in range(LEVELS):
                s = 1 << lv
                g.memset(level_mask[:, lv].rearrange("p (b h j) -> p b h j", h=2, j=s)[:, :, 0, :], 1.0)
            pool.drain()
            for lv in range(LEVELS):
                s = 1 << lv
                v = level_mask[:, lv].rearrange("p (b j) -> p b j", j=2 * s)
                g.affine_select(out=v, in_=v, compare_op=ALU.is_ge, fill=0.0, base=-s,
                                pattern=[[-2 * s, P // (2 * s)], [0, 2 * s]], channel_multiplier=1)
            pool.drain()
            for lv in range(LEVELS):
                s = 1 << lv
                v = level_mask[:, lv].rearrange("p (b j) -> p b j", j=2 * s)
                g.affine_select(out=v, in_=v, compare_op=ALU.is_ge, fill=0.0, base=2 * s - 1,
                                pattern=[[2 * s, P // (2 * s)], [0, 2 * s]], channel_multiplier=-1)
            pool.drain()
            g.tensor_copy(halfmask[:, 1:2], level_mask[:, 4, 0:1])
            for b in range(1, 4):
                pool.drain()
                g.tensor_tensor(halfmask[:, 1:2], halfmask[:, 1:2], level_mask[:, 4, 32 * b:32 * b + 1], ALU.add)
            pool.drain()
            g.tensor_scalar(halfmask[:, 0:1], halfmask[:, 1:2], -1.0, 1.0, ALU.mult, ALU.add).then_inc(const_ready, 1)

            with pool.Fori(0, GROUPS) as gi:
                for c in range(2):
                    if c == 0:
                        pool.wait_ge(prologue_done, gi + 1)
                    g.tensor_copy(ggrp[:, c], glog[:, c, ds(GV * gi, GV)])
                    pool.drain()
                    for a in range(GV):
                        g.tensor_scalar(gU[:, c, a], upper, ggrp[:, c, a:a + 1], None, ALU.mult)
                    pool.drain()
                    pool.sem_inc(gu_ready, 1)
                for m in (Ti, Tt):
                    for c in range(2):
                        g.tensor_copy(m[:, c], ident[:, :].unsqueeze(1).to_broadcast([P, GV, P]))
                for c in range(2):
                    pool.wait_ge(dexp_ready, 2 * gi + c + 1)
                    g.tensor_tensor(Dm[:, c], Dc[:, c], upper.unsqueeze(1).to_broadcast([P, GV, P]), ALU.mult)
                    pool.drain()
                    pool.sem_inc(dm_ready, 1)
                pool.wait_ge(tok_taken, gi + 1)
                kview = kdec.rearrange("p (b r) d -> p b r d", r=2)
                g.tensor_tensor(kview, ktok.unsqueeze(2).to_broadcast([P, GQ, 2, P]),
                                kd[:, ds(GV * gi, GV)].rearrange("p (b r) -> p b r", r=2).unsqueeze(3)
                                .to_broadcast([P, GQ, 2, P]), ALU.mult)
                g.tensor_tensor(qd.rearrange("p (b r) d -> p b r d", r=2),
                                qkT[:, 0, :, P:T].unsqueeze(2).to_broadcast([P, GQ, 2, P]),
                                Eg.rearrange("p (b r) d -> p b r d", r=2), ALU.mult)
                pool.drain()
                pool.sem_inc(aux_ready, 1)
            pool.sem_inc(phase_done[0], 1)

            for i in (1, 2, 3):
                pool.sem_inc(phase_done[i], 1)
            pool.wait_ge(phase_done[2], 4)
            g.iota(rt[:, 4], pattern=[[0, MT], [-1, N_E]], base=N_E, channel_multiplier=0,
                   allow_small_or_imprecise_dtypes=True)
            g.iota(slots1, pattern=[[1, CAP]], base=1, channel_multiplier=0, allow_small_or_imprecise_dtypes=True)
            g.memset(upper, 1.0)
            pool.drain()
            g.affine_select(out=upper, in_=upper, compare_op=ALU.is_ge, fill=0.0, base=0,
                            pattern=[[1, P]], channel_multiplier=-1)
            pool.drain()
            pool.sem_inc(rev_ready, 1)

        @block.tensor
        def _(pe):
            mm, tr = nc.tensor.matmul, nc.tensor.transpose
            pe.wait_ge(pro_loaded, 96)
            pe.wait_ge(const_ready, 1)
            for i in range(8):
                for j in range(4):
                    k, m = 2 * i + j // 2, j % 2
                    last = tr(ps[i][:, j * P:j * P + P], xtok[:, m, k::KD], ident[:, :])
                last.then_inc(xt_ready, 1)
            pe.wait_ge(xt_taken, 8)
            for m in range(MT):
                for k in range(KD):
                    last = mm(ps[0][:, m * 64:m * 64 + 64], xT[:, k, m * P:m * P + P], wbd[:, k, :],
                              start=k == 0, stop=k == KD - 1)
            last.then_inc(bd_ready, 1)
            pe.wait_ge(glog_ready, 1)
            gl2 = small[:, 128:192]
            mm(ps[0][:, 0:64], upper, gl2, start=True, stop=True)
            mm(ps[0][:, 64:96], ones[:, :], glog[:, 0], start=True, stop=True).then_inc(gcum_ready, 1)
            pe.wait_ge(prologue_done, 1)

            def project(arrived, buf, bank, use, rhs):
                part(arrived, buf, bank, use, rhs, 0, 2 * KD)

            def part(arrived, buf, bank, use, rhs, lo, hi):
                if lo == 0:
                    pe.wait_ge(slot_loaded[buf], arrived)
                    pe.wait_ge(bank_taken[bank], use + 1)
                for i in range(lo, hi):
                    ct, k = divmod(i, KD)
                    last = mm(ps[bank][:, ct * T:ct * T + T], ring[:, buf, k, ct * P:ct * P + P], rhs[:, k, :],
                              start=k == 0, stop=k == KD - 1)
                if hi == 2 * KD:
                    last.then_inc(bank_ready[bank], 1)

            with pe.Fori(0, GROUPS) as g:
                for r in range(3):
                    project(16 * (2 * g + 1), r, r, 2 * g, xT)
                pe.wait_ge(sq_ready, g + 1)
                for i in range(2):
                    last = mm(ps[3 + i][:, :], ones[:, :], sq[:, i * 512:i * 512 + 512], start=True, stop=True)
                last.then_inc(ss_ready, 1)
                part(16 * (2 * g + 2), 0, 0, 2 * g + 1, xT, 0, 18)
                pe.wait_ge(qk_ready, g + 1)
                for b in range(GQ):
                    last = tr(ps[5][:, b * P:b * P + P], qkT[:, 1, b, 0:P], ident[:, :])
                last.then_inc(tok_ready, 1)

                def decay_products(c):
                    pe.wait_ge(gu_ready, 2 * g + c + 1)
                    mm(ps[3 + 2 * c][:, :], ones[:, :], gU[:, c].rearrange("p a t -> p (a t)"),
                       start=True, stop=True).then_inc(gb_ready, 1)
                    for i in range(2):
                        for b in range(GQ):
                            last = mm(ps[4 + 2 * c][:, (2 * i + b) * P:(2 * i + b) * P + P],
                                      qkT[:, 1, b, c * P:c * P + P], qkT[:, 1 - i, b, c * P:c * P + P],
                                      start=True, stop=True)
                    last.then_inc(kq_ready, 1)

                def z0(lo, hi):
                    part(16 * (2 * g + 2), 1, 1, 2 * g + 1, xT, lo, hi)

                def z1(lo, hi):
                    part(16 * (2 * g + 2), 2, 2, 2 * g + 1, xT, lo, hi)

                decay_products(0)
                part(16 * (2 * g + 2), 0, 0, 2 * g + 1, xT, 18, 2 * KD)
                pe.wait_ge(tok_taken, g + 1)
                decay_products(1)
                z0(0, 16)
                pe.wait_ge(conv_taken, 4 * g + 6)
                for c in range(2):
                    for a in range(GV):
                        last = tr(ps[7 * c][:, a * P:a * P + P], zvT[:, a, c * P:c * P + P], ident[:, :])
                last.then_inc(tok_ready, 1)
                for lv in range(LEVELS):
                    for c in range(2):
                        pe.wait_ge(t_ready[c], 8 * g + lv + 1)
                        for a in range(GV):
                            last = mm(ps[3 + 2 * c][:, a * P:a * P + P], At[:, c, a], Ti[:, c, a],
                                      start=True, stop=True)
                        last.then_inc(p_ready[c], 1)
                    z0(16 + 2 * lv, 18 + 2 * lv)
                    for c in range(2):
                        pe.wait_ge(pm_ready[c], 7 * g + lv + 1)
                        for a in range(GV):
                            mm(ps[3 + 2 * c][:, a * P:a * P + P], Tt[:, c, a], Pm[:, c, a], start=True, stop=True)
                        for a in range(GV):
                            last = mm(ps[4 + 2 * c][:, a * P:a * P + P], Pm[:, c, a], Tt[:, c, a],
                                      start=True, stop=True)
                        last.then_inc(x_ready[c], 1)
                    if lv == LEVELS - 1:
                        z0(16 + 2 * LEVELS, 2 * KD)
                    else:
                        z1(lv, lv + 1)
                pe.wait_ge(t_ready[0], 8 * g + 8)
                pe.wait_ge(t_ready[1], 8 * g + 8)
                pe.wait_ge(vtok_taken, g + 1)
                for a in range(GV):
                    last = mm(ps[3][:, a * P:a * P + P], Tt[:, 0, a], vtok[:, 0, a], start=True, stop=True)
                last.then_inc(apply_pe, 1)
                z1(6, 10)
                pe.wait_ge(apply_dve, 3 * g + 1)
                pe.wait_ge(aux_ready, g + 1)
                for a in range(GV):
                    last = mm(ps[4][:, a * P:a * P + P], kdec[:, a], vn[:, 0, a], start=True, stop=True)
                last.then_inc(apply_pe, 1)
                for a in range(GV):
                    last = mm(ps[7][:, a * P:a * P + P], vn[:, 0, a], attn[:, 0, a], start=True, stop=True)
                last.then_inc(apply_pe, 1)
                z1(10, 13)
                pe.wait_ge(apply_act, 3 * g + 1)
                for a in range(GV):
                    last = mm(ps[5][:, a * P:a * P + P], qkT[:, 1, a // 2, P:T], Sst[:, a], start=True, stop=True)
                last.then_inc(apply_pe, 1)
                z1(13, 19)
                pe.wait_ge(apply_dve, 3 * g + 2)
                for a in range(GV):
                    last = mm(ps[3][:, a * P:a * P + P], Tt[:, 1, a], R[:, a], start=True, stop=True)
                last.then_inc(apply_pe, 1)
                z1(19, 23)
                pe.wait_ge(apply_dve, 3 * g + 3)
                for a in range(GV):
                    mm(ps[6][:, a * P:a * P + P], Sst[:, a], qd[:, a], start=True, stop=False)
                    last = mm(ps[6][:, a * P:a * P + P], vn[:, 1, a], attn[:, 1, a], start=False, stop=True)
                last.then_inc(apply_pe, 1)
                z1(23, 2 * KD)
                pe.wait_ge(osq_ready, g + 1)
                for i in range(2):
                    last = mm(ps[3 + i][:, :], ones[:, :], sq[:, i * 512:i * 512 + 512], start=True, stop=True)
                last.then_inc(oss_ready, 1)
            pe.wait_ge(o_ready, GROUPS)
            pe.sem_inc(phase_done[0], 1)
            pe.wait_ge(phase_done[0], 4)

            def u_slot(s_div, r, use):
                project(16 * (s_div + 1), (S_U + r) % RING, r % 3, use, xT)

            with pe.Fori(0, 2) as q:
                for r in range(3):
                    u_slot(S_U // RING + q, r, U_USE + q)
            for r in range(6, 8):
                u_slot((S_U + r) // RING, r, U_USE + 2)
            pe.wait_ge(s5_loaded, 16 * 10)
            pe.wait_ge(s5_step, 1)
            for i in range(3):
                last = tr(ps[3][:, i * NJ:i * NJ + NJ], spar[0:NJ, i, :], ident[0:NJ, 0:NJ])
            last.then_inc(s5_tr, 1)
            for w, (src, need) in enumerate(((bwide, 2), (cwide, 3))):
                pe.wait_ge(s5_step, need)
                for c in range(2):
                    for q4 in range(4):
                        n = w * 8 + c * 4 + q4
                        if n >= 4:
                            pe.wait_ge(s5_trc, n - 3)
                        for k in range(4 * q4, 4 * q4 + 4):
                            piece = (bwide[:, c, 4 * k:4 * k + 4, :].rearrange("p j q -> p (j q)") if w == 0
                                     else cwide[:, c, k].rearrange("p g n -> p (g n)"))
                            last = tr(ps[4 + n % 4][:, (k % 4) * P:(k % 4) * P + P], piece, ident[:, :])
                        last.then_inc(s5_tr, 1)
            pe.wait_ge(s5_trc, 16)

            def inputs(ch, r):
                c, kh = divmod(r, 2)
                pe.wait_ge(bu_taken, 4 * ch + r + 1)
                for k in range(8):
                    for i in range(4):
                        last = mm(ps[4 + i][:, k * STEPS:k * STEPS + STEPS],
                                  BT[32 * i:32 * i + 32, c, kh * 8 + k, :],
                                  uch[32 * i:32 * i + 32, kh * 8 + k, :],
                                  start=True, stop=True)
                last.then_inc(bu_ready, 1)

            def chunk(ch, more):
                for r in range(1, 4):
                    inputs(ch, r)
                for h in range(2):
                    project(16 * ((S_DN // RING + 1) + 2 * ch + h), S_DN % RING, 0, DN_USE + 2 * ch + h, xT)
                    pe.wait_ge(bank_taken[1], DN_USE + 2 * ch + h + 1)
                    for half in range(2):
                        buf = (S_DN + 1 + half) % RING
                        pe.wait_ge(slot_loaded[buf], 16 * ((S_DN + 1 + half) // RING + 1 + 2 * ch + h))
                        for ct in range(2):
                            for k in range(KD):
                                last = mm(ps[1][:, ct * T:ct * T + T], ring[:, buf, k, ct * P:ct * P + P],
                                          oT[:, half * KD + k, :], start=half == 0 and ct == 0 and k == 0,
                                          stop=half == 1 and k == KD - 1, skip_group_check=True)
                    last.then_inc(bank_ready[1], 1)
                if more:
                    pe.wait_ge(uch_ready, ch + 2)
                    inputs(ch + 1, 0)
                pe.wait_ge(scan_done, ch + 1)
                pe.wait_ge(y_taken, ch + 1)
                for k in range(KD):
                    for i in range(4):
                        for c in range(2):
                            last = mm(ps[2 + k // 8][32 * i:32 * i + 32, (k % 8) * STEPS:(k % 8) * STEPS + STEPS],
                                      CT[:, c, k, 32 * i:32 * i + 32], SS[:, 1:STEPS + 1, c, 4 * k + i],
                                      start=c == 0, stop=c == 1)
                last.then_inc(y_ready, 1)

            pe.wait_ge(uch_ready, 1)
            inputs(0, 0)
            with pe.Fori(0, NCH - 1) as ch:
                chunk(ch, True)
            chunk(NCH - 1, False)
            pe.sem_inc(phase_done[1], 1)
            pe.wait_ge(gelu_done, 1)

            with pe.Fori(0, 8) as c:
                project(16 * (S_GLU // RING + 1 + c), S_GLU % RING, 0, GLU_USE + c, uT)
                project(16 * ((S_GLU + 1) // RING + 1 + c), (S_GLU + 1) % RING, 1, GLU_USE + c, uT)
                project(16 * ((S_GLU + 2) // RING + 1 + c), (S_GLU + 2) % RING, 2, GS5_USE + c, xT)
            pe.sem_inc(phase_done[2], 1)
            pe.wait_ge(phase_done[2], 4)

            def mix_slot(s16, r, use):
                buf, bank = (S_MIX + r) % RING, 3 + r % 3
                pe.wait_ge(slot_loaded[buf], s16)
                pe.wait_ge(bank_taken[r % 3], use)
                for m in range(MT):
                    for k in range(KD):
                        last = mm(ps[bank][:, m * SC:m * SC + SC], mg[:, k, m * P:m * P + P], ring[:, buf, k, :],
                                  start=k == 0, stop=k == KD - 1)
                last.then_inc(bank_ready[r % 3], 1)

            for r in range(2):
                mix_slot(16 * ((S_MIX + r) // RING + 1), r, MIX_USE[r] + 1)
            with pe.Fori(0, 2) as q:
                for r in range(2, 5):
                    mix_slot(16 * ((S_MIX + r) // RING + 1 + q), r, (MIX_USE[r % 3] + (r // 3) + 1) + q)
            pe.sem_inc(phase_done[3], 1)

            pe.wait_ge(h1_ready, 1)
            for i in range(8):
                for j in range(4):
                    k, m = 2 * i + j // 2, j % 2
                    last = tr(ps[i][:, j * P:j * P + P], h1[:, m, k * P:k * P + P], ident[:, :])
                last.then_inc(ht_ready, 1)
            pe.wait_ge(ht_taken, 8)
            pe.wait_ge(rt_loaded, 64)
            for m in range(MT):
                for k in range(KD):
                    last = mm(ps[0][:, m * N_E:m * N_E + N_E], h1T[:, k, m * P:m * P + P], wr[:, k, :],
                              start=k == 0, stop=k == KD - 1)
            last.then_inc(logit_ready, 1)
            pe.wait_ge(wt_ready, 1)
            for m in range(MT):
                last = tr(ps[1][0:N_E, m * P:m * P + P], wt[:, m], ident[:, :])
            last.then_inc(wtt_ready, 1)
            pe.wait_ge(wtt_taken, 1)
            for m in range(MT):
                for n in range(4):
                    last = mm(ps[(2 + 4 * m + n) % 8][:, :], wtT[:, m * P:m * P + P], bdn[0:N_E, n * 512:n * 512 + 512],
                              start=True, stop=True)
            last.then_inc(bd2_ready, 1)
            pe.wait_ge(acc0_ready, 1)

            sel = rt[:, 6]
            mm(ps[2][:, 0:N_E], upper, sel[:, 0], start=True, stop=True)
            mm(ps[2][:, N_E:2 * N_E], ones[:, :], sel[:, 0], start=True, stop=False)
            mm(ps[2][:, N_E:2 * N_E], upper, sel[:, 1], start=False, stop=True)
            mm(ps[2][:, 2 * N_E:3 * N_E], ones[:, :], sel[:, 0], start=True, stop=False)
            mm(ps[2][:, 2 * N_E:3 * N_E], ones[:, :], sel[:, 1], start=False, stop=True).then_inc(pos_ready, 1)

            def gate(e):
                pe.wait_ge(gw_loaded, 16 * e + 16)
                pe.wait_ge(gate_taken, e + 1)
                for m in range(MT):
                    for k in range(KD):
                        last = mm(ps[m][:, :], h1T[:, k, m * P:m * P + P], GW[:, k, :], start=k == 0, stop=k == KD - 1)
                last.then_inc(gate_done, 1)

            def up(e):
                pe.wait_ge(uw_loaded, 16 * e + 16)
                for m in range(MT):
                    for k in range(KD):
                        last = mm(ps[2 + m][:, :], h1T[:, k, m * P:m * P + P], UW[:, k, :],
                                  start=k == 0, stop=k == KD - 1)
                last.then_inc(up_done, 1)

            def down(e):
                pe.wait_ge(hb_ready, e + 1)
                for m in range(MT):
                    for k in range(KF):
                        last = tr(ps[4 + m][:, k * P:k * P + P], hb[:, m, k::KF], ident[:, :])
                last.then_inc(htr_ready, 1)
                pe.wait_ge(htr_taken, e + 1)
                pe.wait_ge(dw_loaded, 16 * e + 16)
                for n in range(8):
                    pe.wait_ge(dn_taken[n % 2], 4 * e + n // 2 + 1)
                    for k in range(KF):
                        last = mm(ps[6 + n % 2][:, :], hT[:, k, (n // 4) * P:(n // 4) * P + P],
                                  DW[:, k, (n % 4) * 512:(n % 4) * 512 + 512], start=k == 0, stop=k == KF - 1)
                    last.then_inc(dn_ready[n % 2], 1)

            def gather(e):
                pe.wait_ge(p_built, e + 1)
                if not isinstance(e, int):
                    pe.wait_ge(sc_taken, 8 * e - 6)
                for i in range(2):
                    for k in range(8):
                        for m in range(MT):
                            last = mm(ps[i][:, k * CAP:k * CAP + CAP], h1[:, m, (8 * i + k) * P:(8 * i + k) * P + P], Psel[:, m],
                                      start=m == 0, stop=m == MT - 1)
                    last.then_inc(xg_done, 1)

            def expand(bank, w, loaded, e, done, lo=0, hi=KD):
                if lo == 0:
                    pe.wait_ge(loaded, 16 * e + 16)
                for k in range(lo, hi):
                    last = mm(ps[bank][0:CAP, :], xg[:, k, :], w[:, k, :], start=k == 0, stop=k == KD - 1)
                if hi == KD:
                    last.then_inc(done, 1)

            def sgate(e, lo=0, hi=KD):
                if lo == 0:
                    pe.wait_ge(xg_taken, 2 * e + 2)
                    pe.wait_ge(gate_taken, e + 1)
                expand(2, GW, gw_loaded, e, gate_done, lo, hi)

            def sup(e, lo=0, hi=KD):
                expand(3, UW, uw_loaded, e, up_done, lo, hi)

            def sturn(e):
                pe.wait_ge(hb_ready, e + 1)
                pe.sem_inc(turn_begun, 1)
                for m in range(MT):
                    tr(ps[4][0:CAP, 256 + m * P:256 + m * P + P], Pw[:, m], ident[:, :])
                for k in range(KF):
                    last = tr(ps[4][:, k * CAP:k * CAP + CAP], shb[0:CAP, k::KF], ident[0:CAP, 0:CAP])
                last.then_inc(htr_ready, 1)

            def sdown(e):
                pe.wait_ge(htr_taken, e + 1)
                pe.wait_ge(dw_loaded, 16 * e + 16)
                pe.wait_ge(sc_taken, 8 * e + 4)
                for n in range(4):
                    pe.wait_ge(y_copied, 4 * e + n + 1)
                    for k in range(KF):
                        last = mm(ps[5 + n % 2][0:CAP, :], shT[:, k, :], DW[:, k, n * 512:n * 512 + 512],
                                  start=k == 0, stop=k == KF - 1)
                    last.then_inc(sdn_done, 1)

            def scatter(e, lo, hi):
                if lo == 0:
                    pe.wait_ge(y_copied, 4 * e + 6)
                for n in range(lo, hi):
                    pe.wait_ge(sc_taken, 8 * e + n + 1)
                    last = mm(ps[(0, 1, 6, 7)[n % 4]][:, :], pwT[0:CAP, (n // 4) * P:(n // 4) * P + P],
                              ysb[0:CAP, (n % 4) * 512:(n % 4) * 512 + 512], start=True, stop=True)
                    last.then_inc(sc_done, 1)

            def sparse(e, more):
                sgate(e, 0, 14)
                sturn(e - 1)
                sgate(e, 14, KD)
                sdown(e - 1)
                sup(e, 0, 8)
                scatter(e - 1, 0, 4)
                sup(e, 8, 12)
                scatter(e - 1, 4, 6)
                sup(e, 12, KD)
                if more:
                    gather(e + 1)
                scatter(e - 1, 6, 8)

            pe.wait_ge(flag_ready, 1)
            over = pe.value_load(flag[0:1, 0:1], min_val=0, max_val=1)
            with pe.If(over < 1):
                gather(0)
                sgate(0)
                sup(0)
                gather(1)
                with pe.Fori(1, N_E - 1) as e:
                    sparse(e, True)
                sparse(N_E - 1, False)
                sturn(N_E - 1)
                sdown(N_E - 1)
                scatter(N_E - 1, 0, 8)
            with pe.If(over > 0):
                gate(0)
                up(0)
                with pe.Fori(1, N_E) as e:
                    gate(e)
                    down(e - 1)
                    up(e)
                down(N_E - 1)

        @block.scalar
        def _(act):
            A = nc.scalar.activation
            for i in range(0, 8, 2):
                act.wait_ge(xt_ready, i + 1)
                nc.scalar.copy(xT[:, 2 * i:2 * i + 2, :], ps[i][:, :].rearrange("p (k t) -> p k t", k=2)).then_inc(xt_taken, 1)
            act.wait_ge(bd_ready, 1)
            bd = ps[0][:, 0:128].rearrange("p (m c) -> p m c", m=2)
            act.wait_ge(sp_in, 1)
            A(beta, bd[:, :, 0:32], ACT.Sigmoid)
            A(sp0[:, 0], sp0[:, 0], ACT.Exp)
            A(arow, arow, ACT.Exp)
            act.drain()
            A(sp0[:, 0], sp0[:, 0], ACT.Ln, bias=1.0)
            act.drain()
            act.sem_inc(sp_done, 1)
            act.wait_ge(kd_in, 1)
            A(neg_eg, gcum[:, 1], ACT.Exp)
            A(kd, kd, ACT.Exp)
            act.drain()
            act.sem_inc(kd_out, 1)

            with act.Fori(0, GROUPS) as g:
                def silu(r):
                    act.wait_ge(conv_ready, 4 * g + r + 1)
                    dst = qkT[:, r] if r < 2 else zvT[:, 2 * (r - 2):2 * (r - 2) + 2]
                    A(dst, cv[:, r % 2].rearrange("p (h t) -> p h t", h=2), ACT.Silu).then_inc(conv_taken, 1)

                silu(0)
                silu(1)
                act.drain()
                A(sq, qkT.rearrange("p i h t -> p (i h t)"), ACT.Square).then_inc(sq_ready, 1)
                act.wait_ge(ss_ready, g + 1)
                for i in range(2):
                    A(rn[:, i * 512:i * 512 + 512], ps[3 + i][:, :], ACT.Ln, bias=eps_l2)
                act.drain()
                A(rn[:, 0:512], rn[:, 0:512], ACT.Exp, scale=-0.5, bias=lnq)
                A(rn[:, 512:1024], rn[:, 512:1024], ACT.Exp, scale=-0.5).then_inc(rn_ready, 1)
                silu(2)
                act.wait_ge(arg_ready, 2 * g + 1)
                A(Dc[:, 0], Dc[:, 0], ACT.Exp)
                act.drain()
                act.sem_inc(dexp_ready, 1)
                silu(3)
                act.wait_ge(arg_ready, 2 * g + 2)
                A(Eg, ps[5][:, :].rearrange("p (a t) -> p a t", a=GV), ACT.Exp)
                A(Dc[:, 1], Dc[:, 1], ACT.Exp)
                act.drain()
                act.sem_inc(dexp_ready, 1)
                act.wait_ge(tok_ready, 2 * g + 2)
                for c in range(2):
                    last = nc.scalar.copy(vtok[:, c], ps[7 * c][:, :].rearrange("p (a d) -> p a d", a=GV))
                last.then_inc(vtok_taken, 1)
                act.wait_ge(bank_ready[1], 2 * g + 2)
                A(zs[:, 0:2], ps[1][:, :].rearrange("p (h t) -> p h t", h=2), ACT.Silu).then_inc(bank_taken[1], 1)
                act.wait_ge(apply_pe, 6 * g + 2)
                nc.scalar.copy(Sst, ps[4][:, :].rearrange("p (a d) -> p a d", a=GV)).then_inc(apply_act, 1)
                act.wait_ge(apply_pe, 6 * g + 3)
                nc.scalar.copy(oT[:, ds(GV * g, GV), 0:P], ps[7][:, :].rearrange("p (a t) -> p a t", a=GV)).then_inc(apply_act, 1)
                act.wait_ge(apply_pe, 6 * g + 6)
                nc.scalar.copy(oT[:, ds(GV * g, GV), P:T], ps[6][:, :].rearrange("p (a t) -> p a t", a=GV)).then_inc(apply_act, 1)
                act.drain()
                A(sq.rearrange("p (a t) -> p a t", a=GV), oT[:, ds(GV * g, GV), :], ACT.Square).then_inc(osq_ready, 1)
                act.wait_ge(bank_ready[2], 2 * g + 2)
                A(zs[:, 2:4], ps[2][:, :].rearrange("p (h t) -> p h t", h=2), ACT.Silu).then_inc(bank_taken[2], 1)
                act.wait_ge(oss_ready, g + 1)
                for i in range(2):
                    A(rn[:, i * 512:i * 512 + 512], ps[3 + i][:, :], ACT.Ln, scale=1.0 / P, bias=eps_l2)
                act.drain()
                A(rn, rn, ACT.Exp, scale=-0.5).then_inc(orn_ready, 1)
            act.sem_inc(phase_done[0], 1)
            act.wait_ge(phase_done[0], 4)

            def take_u(bank, use, k):
                act.wait_ge(bank_ready[bank], use + 1)
                nc.scalar.copy(uT[:, k, :], ps[bank][:, :].rearrange("p (k t) -> p k t", k=2)).then_inc(bank_taken[bank], 1)

            with act.Fori(0, 2) as q:
                for r in range(3):
                    take_u(r, U_USE + q, ds(6 * q + 2 * r, 2))
            for r in range(6, 8):
                take_u(r % 3, U_USE + 2, slice(2 * r, 2 * r + 2))
            act.wait_ge(s5_dve, 1)
            A(coef[:, 2], coef[:, 2], ACT.Exp)
            act.drain()
            act.sem_inc(s5_act, 1)
            act.wait_ge(s5_dve, 2)
            A(coef[:, 3], coef[:, 3], ACT.Exp)
            A(coef[:, 4], coef[:, 4], ACT.Sin)
            A(coef[:, 5], coef[:, 5], ACT.Sin)
            act.drain()
            act.sem_inc(s5_act, 1)
            for n in range(0, 16):
                act.wait_ge(s5_tr, n + 2)
                dst = (BT if n < 8 else CT)[:, (n // 4) % 2, 4 * (n % 4):4 * (n % 4) + 4, :]
                src = ps[4 + n % 4][:, :].rearrange("p (k m) -> p k m", k=4)
                if n >= 12:
                    A(dst, src, ACT.Copy, scale=-1.0).then_inc(s5_trc, 1)
                else:
                    nc.scalar.copy(dst, src).then_inc(s5_trc, 1)
            act.sem_inc(bu_taken, 1)
            act.sem_inc(y_ready, 1)
            view = SS[:, 1:STEPS + 1].rearrange("p t c (h k i) -> p h c i k t", h=2, i=4)
            with act.Fori(0, NCH) as ch:
                for c in range(2):
                    for kh in range(2):
                        act.wait_ge(bu_ready, 4 * ch + 2 * c + kh + 1)
                        if c == kh == 0:
                            act.wait_ge(y_ready, ch + 1)
                        for i in range(4):
                            nc.scalar.copy(view[:, kh, c, i], ps[4 + i][:, :].rearrange("p (k t) -> p k t", k=8))
                        act.drain()
                        act.sem_inc(bu_taken, 1)
                act.sem_inc(chunk_filled, 1)
                for h in range(2):
                    act.wait_ge(bank_ready[0], DN_USE + 1 + 2 * ch + h)
                    act.wait_ge(merged_ready, 2 * ch + h + 1)
                    A(gdt, ps[0][:, :], ACT.Sigmoid)
                    act.drain()
                    act.sem_inc(bank_taken[0], 1)
                    act.sem_inc(gd_ready, 1)
            act.sem_inc(phase_done[1], 1)
            act.wait_ge(y_taken, NCH + 1)
            for i in range(4):
                last = A(uT[:, 4 * i:4 * i + 4], uT[:, 4 * i:4 * i + 4], ACT.Gelu_apprx_tanh)
            act.drain()
            act.sem_inc(gelu_done, 1)
            with act.Fori(0, 8) as c:
                act.wait_ge(glu_used, c + 1)
                act.wait_ge(bank_ready[1], GLU_USE + c + 1)
                A(ta, ps[1][:, :], ACT.Sigmoid).then_inc(bank_taken[1], 1)
                act.wait_ge(bank_ready[2], GS5_USE + 1 + c)
                A(tb, ps[2][:, :], ACT.Sigmoid).then_inc(bank_taken[2], 1)
                act.drain()
                act.sem_inc(glu_ready, 1)
            act.sem_inc(phase_done[2], 1)
            act.sem_inc(phase_done[3], 1)
            for m in range(MT):
                act.wait_ge(ln_step, m + 1)
                v = stats[:, 50:51]
                A(v, v, ACT.Ln, bias=eps_ln)
                act.drain()
                A(v, v, ACT.Exp, scale=-0.5)
                act.drain()
                act.sem_inc(ln_act, 1)
            for i in range(0, 8, 2):
                act.wait_ge(ht_ready, i + 1)
                nc.scalar.copy(h1T[:, 2 * i:2 * i + 2, :], ps[i][:, :].rearrange("p (k t) -> p k t", k=2)).then_inc(ht_taken, 1)
            for r in range(TOP_K):
                act.wait_ge(rexp_in, r + 1)
                A(rm[:, 4 + r], rm[:, 4 + r], ACT.Exp).then_inc(rexp_out, 1)

            def hidden(e):
                act.wait_ge(gate_taken, e + 2)
                A(sg, gb, ACT.Sigmoid, scale=SW_ALPHA).then_inc(sig_ready, 1)

            def turn(e):
                act.wait_ge(htr_ready, e + 1)
                for m in range(MT):
                    last = nc.scalar.copy(hT[:, :, m * P:m * P + P], ps[4 + m][:, :].rearrange("p (k t) -> p k t", k=KF))
                last.then_inc(htr_taken, 1)

            def sgather(e):
                for i in range(2):
                    act.wait_ge(xg_done, 2 * e + i + 1)
                    nc.scalar.copy(xg[:, 8 * i:8 * i + 8, :], ps[i][:, :].rearrange("p (k t) -> p k t", k=8)).then_inc(xg_taken, 1)

            def shidden(e):
                act.wait_ge(gate_taken, e + 2)
                A(ssg[0:CAP], sgb[0:CAP], ACT.Sigmoid, scale=SW_ALPHA).then_inc(sig_ready, 1)

            def sturn(e):
                act.wait_ge(htr_ready, e + 1)
                nc.scalar.copy(shT, ps[4][:, 0:KF * CAP].rearrange("p (k t) -> p k t", k=KF))
                nc.scalar.copy(pwT[0:CAP], ps[4][0:CAP, 256:512]).then_inc(htr_taken, 1)

            def sdown(e):
                for n in range(4):
                    act.wait_ge(sdn_done, 4 * e + n + 1)
                    nc.scalar.copy(ysb[0:CAP, n * 512:n * 512 + 512], ps[5 + n % 2][0:CAP, :]).then_inc(y_copied, 1)

            act.wait_ge(flag_ready, 1)
            over = act.value_load(flag[0:1, 0:1], min_val=0, max_val=1)
            with act.If(over < 1):
                act.sem_inc(y_copied, 2)
                sgather(0)
                shidden(0)
                sgather(1)
                with act.Fori(1, N_E - 1) as e:
                    sturn(e - 1)
                    shidden(e)
                    sdown(e - 1)
                    sgather(e + 1)
                sturn(N_E - 2)
                shidden(N_E - 1)
                sdown(N_E - 2)
                sturn(N_E - 1)
                sdown(N_E - 1)
            with act.If(over > 0):
                hidden(0)
                with act.Fori(1, N_E) as e:
                    hidden(e)
                    turn(e - 1)
                turn(N_E - 1)
            for m in range(MT):
                act.wait_ge(ln_step, MT + m + 1)
                v = stats[:, 50:51]
                A(v, v, ACT.Ln, bias=eps_ln)
                act.drain()
                A(v, v, ACT.Exp, scale=-0.5)
                act.drain()
                act.sem_inc(ln_act, 1)

        @block.vector
        def _(dve):
            V = nc.vector
            for b in range(3):
                dve.sem_inc(bank_taken[b], 1)
            dve.sem_inc(conv_taken, 2)
            for i in range(1, 8, 2):
                dve.wait_ge(xt_ready, i + 1)
                V.tensor_copy(xT[:, 2 * i:2 * i + 2, :], ps[i][:, :].rearrange("p (k t) -> p k t", k=2)).then_inc(xt_taken, 1)
            dve.wait_ge(bd_ready, 1)
            bd = ps[0][:, 0:128].rearrange("p (m c) -> p m c", m=2)
            V.tensor_tensor(sp0[:, 1], bd[:, :, 32:64], dtrow.unsqueeze(1).to_broadcast([P, 2, 32]), ALU.add)
            dve.drain()
            V.scalar_tensor_tensor(out=sp0[:, 0], in0=sp0[:, 1], scalar=-1.0, in1=sp0[:, 1], op0=ALU.mult, op1=ALU.min)
            dve.drain()
            dve.sem_inc(sp_in, 1)
            dve.wait_ge(sp_done, 1)
            V.scalar_tensor_tensor(out=sp0[:, 1], in0=sp0[:, 1], scalar=0.0, in1=sp0[:, 0], op0=ALU.max, op1=ALU.add)
            dve.drain()
            V.scalar_tensor_tensor(out=glog, in0=sp0[:, 1], scalar=-1.0,
                                   in1=arow.unsqueeze(1).to_broadcast([P, 2, 32]), op0=ALU.mult, op1=ALU.mult)
            dve.drain()
            dve.sem_inc(glog_ready, 1)
            dve.wait_ge(gcum_ready, 1)
            V.tensor_copy(gcum, ps[0][:, 0:64].rearrange("p (m c) -> p m c", m=2))
            dve.drain()
            V.tensor_tensor(kd, ps[0][:, 64:96], gcum[:, 0], ALU.subtract)
            dve.drain()
            dve.sem_inc(kd_in, 1)
            dve.wait_ge(kd_out, 1)
            V.tensor_scalar(neg_eg, neg_eg, -1.0, None, ALU.mult)
            dve.drain()
            dve.sem_inc(prologue_done, 1)

            with dve.Fori(0, GROUPS) as g:
                def conv(r):
                    tile = (GQ * g, H_QK + GQ * g, 2 * H_QK + GV * g, 2 * H_QK + 2 + GV * g)[r]
                    dve.wait_ge(bank_ready[r % 3], 2 * g + r // 3 + 1)
                    dve.wait_ge(conv_taken, 4 * g + r + 1)
                    for ct in range(2):
                        V.tensor_scalar(cv[:, r % 2, ct * T:ct * T + T], ps[r % 3][:, ct * T:ct * T + T],
                                        cw[:, ds(tile + ct, 1), 3:4].rearrange("p a b -> p (a b)"), None, ALU.mult)
                    dve.drain()
                    for sh in range(1, 4):
                        for ct in range(2):
                            dst = cv[:, r % 2, ct * T + sh:ct * T + T]
                            V.scalar_tensor_tensor(out=dst, in0=ps[r % 3][:, ct * T:ct * T + T - sh],
                                                   scalar=cw[:, ds(tile + ct, 1), 3 - sh:4 - sh].rearrange("p a b -> p (a b)"),
                                                   in1=dst, op0=ALU.mult, op1=ALU.add)
                        dve.drain()
                    dve.sem_inc(bank_taken[r % 3], 1)
                    dve.sem_inc(conv_ready, 1)

                def decay(c):
                    dve.wait_ge(gb_ready, 2 * g + c + 1)
                    for a in range(GV):
                        V.tensor_scalar(Dc[:, c, a], ps[3 + 2 * c][:, a * P:a * P + P],
                                        gcum[:, c, ds(GV * g + a, 1)], 0.0, ALU.subtract, ALU.min)
                    dve.drain()
                    dve.sem_inc(arg_ready, 1)

                conv(0)
                conv(1)
                conv(2)
                dve.wait_ge(rn_ready, g + 1)
                V.tensor_tensor(qkT.rearrange("p i h t -> p (i h t)"), qkT.rearrange("p i h t -> p (i h t)"), rn,
                                ALU.mult).then_inc(qk_ready, 1)
                dve.wait_ge(tok_ready, 2 * g + 1)
                V.tensor_copy(ktok, ps[5][:, 0:GQ * P].rearrange("p (b d) -> p b d", b=GQ)).then_inc(tok_taken, 1)
                decay(0)
                conv(3)
                decay(1)
                for c in range(2):
                    dve.wait_ge(kq_ready, 2 * g + c + 1)
                    dve.wait_ge(dm_ready, 2 * g + c + 1)
                    for a in range(GV):
                        V.scalar_tensor_tensor(out=At[:, c, a], in0=ps[4 + 2 * c][:, (a // 2) * P:(a // 2) * P + P],
                                               scalar=beta[:, c, ds(GV * g + a, 1)], in1=Dc[:, c, a],
                                               op0=ALU.mult, op1=ALU.mult)
                    V.tensor_tensor(attn[:, c].rearrange("p (b r) t -> p b r t", r=2),
                                    ps[4 + 2 * c][:, 2 * P:4 * P].rearrange("p (b t) -> p b t", b=2).unsqueeze(2)
                                    .to_broadcast([P, GQ, 2, P]),
                                    Dm[:, c].rearrange("p (b r) t -> p b r t", r=2), ALU.mult)
                    dve.drain()
                    dve.sem_inc(t_ready[c], 1)
                for lv in range(LEVELS):
                    for c in range(2):
                        dve.wait_ge(p_ready[c], 7 * g + lv + 1)
                        V.tensor_tensor(Pm[:, c], ps[3 + 2 * c][:, :].rearrange("p (a t) -> p a t", a=GV),
                                        level_mask[:, lv:lv + 1, :].to_broadcast([P, GV, P]), ALU.mult).then_inc(pm_ready[c], 1)
                    for c in range(2):
                        dve.wait_ge(x_ready[c], 7 * g + lv + 1)
                        V.tensor_tensor(Ti[:, c], Ti[:, c], ps[3 + 2 * c][:, :].rearrange("p (a t) -> p a t", a=GV),
                                        ALU.subtract)
                        V.tensor_tensor(Tt[:, c], Tt[:, c], ps[4 + 2 * c][:, :].rearrange("p (a t) -> p a t", a=GV),
                                        ALU.subtract)
                        dve.drain()
                        dve.sem_inc(t_ready[c], 1)

                def by_head(v, width):
                    return v.unsqueeze(2).to_broadcast([P, GV, width])

                dve.wait_ge(apply_pe, 6 * g + 1)
                V.tensor_tensor(vn[:, 0], ps[3][:, :].rearrange("p (a d) -> p a d", a=GV),
                                by_head(beta[:, 0, ds(GV * g, GV)], P), ALU.mult).then_inc(apply_dve, 1)
                dve.wait_ge(apply_pe, 6 * g + 4)
                V.tensor_tensor(R, ps[5][:, :].rearrange("p (a d) -> p a d", a=GV),
                                by_head(neg_eg[:, ds(GV * g, GV)], P), ALU.mult)
                dve.drain()
                V.tensor_tensor(R, R, vtok[:, 1], ALU.add).then_inc(apply_dve, 1)
                dve.wait_ge(apply_pe, 6 * g + 5)
                V.tensor_tensor(vn[:, 1], ps[3][:, :].rearrange("p (a d) -> p a d", a=GV),
                                by_head(beta[:, 1, ds(GV * g, GV)], P), ALU.mult).then_inc(apply_dve, 1)
                dve.wait_ge(orn_ready, g + 1)
                og = oT[:, ds(GV * g, GV), :]
                V.tensor_tensor(og, og, rn.rearrange("p (a t) -> p a t", a=GV), ALU.mult)
                dve.drain()
                dve.wait_ge(bank_taken[2], 2 * g + 3)
                V.scalar_tensor_tensor(out=og, in0=og, scalar=normw, in1=zs, op0=ALU.mult, op1=ALU.mult)
                dve.drain()
                dve.sem_inc(o_ready, 1)
                dve.sem_inc(prologue_done, 1)
            dve.sem_inc(phase_done[0], 1)
            dve.wait_ge(phase_done[0], 4)

            dve.wait_ge(s5_loaded, 160)
            V.tensor_copy(spar[0:NJ, 2, :].rearrange("p (g n) -> p g n", g=2),
                          coef[0:NJ, 15, 0:2].unsqueeze(2).to_broadcast([NJ, 2, 64]))
            dve.drain()
            dve.sem_inc(s5_step, 1)
            dve.wait_ge(s5_tr, 1)
            LRE, LIM, DT, MAG, SIN, COS, ARE, AIM, NUM, DEN, FRE, FIM, X1, X2 = (coef[:, i] for i in range(14))
            V.tensor_scalar(LRE, ps[3][:, 0:NJ], -1e-4, None, ALU.min)
            V.tensor_copy(LIM, ps[3][:, NJ:2 * NJ])
            V.tensor_copy(DT, ps[3][:, 2 * NJ:3 * NJ])
            dve.drain()
            dve.sem_inc(s5_dve, 1)
            dve.wait_ge(s5_act, 1)

            V.tensor_tensor(MAG, LRE, DT, ALU.mult)
            V.tensor_tensor(X1, LIM, DT, ALU.mult)
            dve.drain()
            V.tensor_scalar(itmp[:, :], X1, 1.0 / TWO_PI, None, ALU.mult)
            dve.drain()
            V.tensor_copy(X2, itmp[:, :])
            dve.drain()
            V.scalar_tensor_tensor(out=X1, in0=X2, scalar=-TWO_PI_HI, in1=X1, op0=ALU.mult, op1=ALU.add)
            dve.drain()
            V.scalar_tensor_tensor(out=X1, in0=X2, scalar=-TWO_PI_LO, in1=X1, op0=ALU.mult, op1=ALU.add)
            dve.drain()
            V.tensor_scalar(SIN, X1, PI_SAFE, -PI_SAFE, ALU.min, ALU.max)
            V.tensor_scalar(X1, X1, math.pi / 2, None, ALU.add)
            dve.drain()
            V.tensor_scalar(X2, X1, math.pi, -TWO_PI, ALU.is_gt, ALU.mult)
            dve.drain()
            V.tensor_tensor(X1, X1, X2, ALU.add)
            dve.drain()
            V.tensor_scalar(COS, X1, PI_SAFE, -PI_SAFE, ALU.min, ALU.max)
            dve.drain()
            dve.sem_inc(s5_dve, 1)
            dve.wait_ge(s5_act, 2)
            V.tensor_tensor(ARE, MAG, COS, ALU.mult)
            V.tensor_tensor(AIM, MAG, SIN, ALU.mult)
            V.tensor_tensor(X1, LRE, LRE, ALU.mult)
            V.tensor_tensor(X2, LIM, LIM, ALU.mult)
            dve.drain()
            V.tensor_tensor(DEN, X1, X2, ALU.add)
            V.tensor_copy(Arr, ARE.unsqueeze(1).to_broadcast([P, 2, NJ]))
            V.tensor_copy(Aim[:, 1], AIM)
            V.tensor_scalar(Aim[:, 0], AIM, -1.0, None, ALU.mult)
            dve.drain()
            V.reciprocal(X2, DEN)
            V.tensor_scalar(NUM, ARE, -1.0, None, ALU.add)
            dve.drain()
            V.tensor_tensor(FRE, NUM, LRE, ALU.mult)
            V.tensor_tensor(X1, AIM, LIM, ALU.mult)
            dve.drain()
            V.tensor_tensor(FRE, FRE, X1, ALU.add)
            V.tensor_tensor(FIM, AIM, LRE, ALU.mult)
            V.tensor_tensor(DEN, NUM, LIM, ALU.mult)
            dve.drain()
            V.tensor_tensor(FIM, FIM, DEN, ALU.subtract)
            V.tensor_tensor(FRE, FRE, X2, ALU.mult)
            dve.drain()
            V.tensor_tensor(FIM, FIM, X2, ALU.mult)
            V.memset(bwide, 0.0)
            dve.drain()
            fr = FRE.unsqueeze(2).to_broadcast([P, NJ, 16])
            fi = FIM.unsqueeze(2).to_broadcast([P, NJ, 16])
            for c, (p1, p2, op) in enumerate(((0, 1, ALU.subtract), (1, 0, ALU.add))):
                V.tensor_tensor(bb[:, c], braw[:, p1], fr, ALU.mult)
                V.tensor_tensor(bt1, braw[:, p2], fi, ALU.mult)
                dve.drain()
                for g2 in range(2):
                    h = slice(64 * g2, 64 * g2 + 64)
                    V.tensor_tensor(bwide[h, c, :, 16 * g2:16 * g2 + 16], bb[h, c], bt1[h], op)
                dve.drain()
            dve.sem_inc(s5_step, 1)
            for c in range(2):
                for g2 in range(2):
                    V.tensor_scalar(cwide[:, c, :, g2, :], craw[:, c], halfmask[:, g2:g2 + 1], None, ALU.mult)
            dve.drain()
            dve.sem_inc(s5_step, 1)
            dve.wait_ge(s5_trc, 16)
            V.memset(SS[:, 0], 0.0)
            dve.drain()
            dve.sem_inc(y_taken, 1)
            dve.sem_inc(merged_ready, 1)

            def take_chunk(ch):
                V.tensor_copy(uch, uT[:, :, ds(STEPS * ch, STEPS)]).then_inc(uch_ready, 1)

            def chunk(ch, more):
                dve.wait_ge(chunk_filled, ch + 1)
                dve.sem_inc(scan_begun, 1)
                if more:
                    take_chunk(ch + 1)
                for h in range(2):
                    with dve.Fori(h * STEPS // 16, (h + 1) * STEPS // 16) as t8:
                        some = SS[:, ds(8 * t8, 9)]
                        for t in range(8):
                            prev, cur = some[:, t], some[:, t + 1]
                            V.tensor_tensor(m1, Arr, prev, ALU.mult)
                            V.tensor_tensor(m2[:, 0], Aim[:, 0], prev[:, 1], ALU.mult)
                            V.tensor_tensor(m2[:, 1], Aim[:, 1], prev[:, 0], ALU.mult)
                            dve.drain()
                            V.tensor_tensor(cur, cur, m1, ALU.add)
                            dve.drain()
                            V.tensor_tensor(cur, cur, m2, ALU.add)
                            dve.drain()
                    if h == 1:
                        V.tensor_copy(SS[:, 0], SS[:, STEPS])
                        dve.drain()
                        dve.sem_inc(scan_done, 1)
                    dve.wait_ge(bank_ready[1], DN_USE + 1 + 2 * ch + h)
                    dve.wait_ge(gd_ready, 2 * ch + h + 1)
                    V.tensor_tensor(mg[:, ds(4 * ch + 2 * h, 2), :], ps[1][:, :].rearrange("p (k t) -> p k t", k=2),
                                    gdt.rearrange("p (k t) -> p k t", k=2), ALU.mult)
                    dve.drain()
                    dve.sem_inc(bank_taken[1], 1)
                    dve.sem_inc(merged_ready, 1)
                dve.wait_ge(y_ready, ch + 2)
                for kh in range(2):
                    uv = uT[:, kh * 8:kh * 8 + 8, ds(STEPS * ch, STEPS)]
                    V.tensor_tensor(ytmp, uv, dsk[:, kh * 8:kh * 8 + 8].unsqueeze(2).to_broadcast([P, 8, STEPS]), ALU.mult)
                    dve.drain()
                    V.tensor_tensor(uv, ytmp, ps[2 + kh][:, :].rearrange("p (k t) -> p k t", k=8), ALU.add)
                    dve.drain()
                dve.sem_inc(y_taken, 1)

            take_chunk(0)
            with dve.Fori(0, NCH - 1) as ch:
                chunk(ch, True)
            chunk(NCH - 1, False)
            dve.sem_inc(phase_done[1], 1)
            dve.wait_ge(phase_done[1], 4)
            dve.sem_inc(glu_used, 1)
            with dve.Fori(0, 8) as c:
                dve.wait_ge(glu_ready, c + 1)
                dve.wait_ge(bank_ready[0], GLU_USE + c + 1)
                V.tensor_tensor(ta, ta, ps[0][:, :], ALU.mult)
                dve.drain()
                dve.sem_inc(bank_taken[0], 1)
                V.tensor_tensor(ta, ta, tb, ALU.mult)
                dve.drain()
                mv = mg[:, ds(2 * c, 2), :]
                V.tensor_tensor(mv, mv, ta.rearrange("p (k t) -> p k t", k=2), ALU.add)
                dve.drain()
                dve.sem_inc(glu_used, 1)
            dve.sem_inc(phase_done[2], 1)

            dve.wait_ge(x_loaded, 16)

            def take_mix(r, use, cols):
                dve.wait_ge(bank_ready[r % 3], use)
                hv = h1[:, :, cols]
                V.scalar_tensor_tensor(out=hv, in0=hv, scalar=ALPHA, in1=ps[3 + r % 3][:, :].rearrange("p (m n) -> p m n", m=2),
                                       op0=ALU.mult, op1=ALU.add)
                dve.drain()
                dve.sem_inc(bank_taken[r % 3], 1)

            for r in range(2):
                take_mix(r, MIX_USE[r] + 1, slice(SC * r, SC * r + SC))
            with dve.Fori(0, 2) as q:
                for r in range(2, 5):
                    take_mix(r, MIX_USE[r % 3] + r // 3 + 1 + q, ds(768 * q + SC * r, SC))
            dve.wait_ge(ln_loaded, 32)

            def norm(m, rows, n):
                for i in range(4):
                    V.bn_stats(stats[:, 6 * i:6 * i + 6], h1[:, m, 512 * i:512 * i + 512])
                dve.drain()
                V.bn_aggr(stats[:, 49:51], stats[:, 0:24])
                dve.drain()
                dve.sem_inc(ln_step, 1)
                dve.wait_ge(ln_act, n + 1)
                V.tensor_scalar(h1[:, m], h1[:, m], stats[:, 49:50], stats[:, 50:51], ALU.subtract, ALU.mult)
                dve.drain()
                V.tensor_tensor(h1[:, m], h1[:, m], rows[:, 0], ALU.mult)
                dve.drain()
                V.tensor_tensor(h1[:, m], h1[:, m], rows[:, 1], ALU.add)
                dve.drain()

            for m in range(MT):
                norm(m, lnrow, m)
            dve.sem_inc(h1_ready, 1)
            dve.sem_inc(phase_done[3], 1)
            for i in range(1, 8, 2):
                dve.wait_ge(ht_ready, i + 1)
                V.tensor_copy(h1T[:, 2 * i:2 * i + 2, :], ps[i][:, :].rearrange("p (k t) -> p k t", k=2)).then_inc(ht_taken, 1)

            lg, eq, oh, rev = rt[:, 1], rt[:, 2], rt[:, 3], rt[:, 4]
            dve.wait_ge(rt_loaded, 64)
            dve.wait_ge(logit_ready, 1)
            V.tensor_tensor(lg, ps[0][:, 0:MT * N_E].rearrange("p (m e) -> p m e", m=MT), rt[:, 7], ALU.add)
            sel = rt[:, 6]
            V.memset(wt, 0.0)
            V.memset(sel, 0.0)
            dve.wait_ge(rev_ready, 1)
            dve.drain()

            def wide(v):
                return v.unsqueeze(2).to_broadcast([P, MT, N_E])

            for r in range(TOP_K):
                V.tensor_reduce(rm[:, r], lg, AX_X, ALU.max)
                dve.drain()
                V.tensor_tensor(rm[:, 4 + r], rm[:, r], rm[:, 0], ALU.subtract)
                V.tensor_tensor(eq, lg, wide(rm[:, r]), ALU.is_equal)
                dve.drain()
                dve.sem_inc(rexp_in, 1)
                V.tensor_tensor(eq, eq, rev, ALU.mult)
                dve.drain()
                V.tensor_reduce(rt[:, 5, :, 0:1].rearrange("p m o -> p (m o)"), eq, AX_X, ALU.max)
                dve.drain()
                V.tensor_tensor(oh, eq, rt[:, 5, :, 0:1].to_broadcast([P, MT, N_E]), ALU.is_equal)
                dve.drain()
                V.scalar_tensor_tensor(out=lg, in0=oh, scalar=-3.0e38, in1=lg, op0=ALU.mult, op1=ALU.add)
                V.tensor_tensor(sel, sel, oh, ALU.add)
                dve.wait_ge(rexp_out, r + 1)
                dve.drain()
                V.tensor_tensor(oh, oh, wide(rm[:, 4 + r]), ALU.mult)
                dve.drain()
                V.tensor_tensor(wt, wt, oh, ALU.add)
                dve.drain()
            V.tensor_reduce(rm[:, 0], wt, AX_X, ALU.add)
            dve.drain()
            V.reciprocal(rm[:, 1], rm[:, 0])
            dve.drain()
            V.tensor_tensor(wt, wt, wide(rm[:, 1]), ALU.mult)
            dve.drain()
            dve.sem_inc(wt_ready, 1)
            dve.wait_ge(wtt_ready, 1)
            V.tensor_copy(wtT[:, :], ps[1][0:N_E, 0:T]).then_inc(wtt_taken, 1)
            dve.wait_ge(bd2_ready, 1)
            for m in range(MT):
                for n in range(4):
                    V.tensor_copy(acc[:, m, n * 512:n * 512 + 512], ps[(2 + 4 * m + n) % 8][:, :])
            dve.drain()
            dve.sem_inc(acc0_ready, 1)
            pos = rt[:, 5]
            dve.wait_ge(pos_ready, 1)
            V.tensor_copy(pos, ps[2][:, 0:MT * N_E].rearrange("p (m e) -> p m e", m=MT))
            V.tensor_reduce(rm[:, 0, 0:1], ps[2][:, 2 * N_E:3 * N_E], AX_X, ALU.max)
            dve.drain()
            V.tensor_scalar(flag[:, :], rm[:, 0, 0:1], CAP + 0.5, None, ALU.is_gt)
            dve.drain()
            dve.sem_inc(flag_ready, 1)
            dve.sem_inc(gate_taken, 1)
            for b in range(2):
                dve.sem_inc(dn_taken[b], 1)

            def take_gate(e):
                dve.wait_ge(gate_done, e + 1)
                dve.wait_ge(brow_loaded, 32 * e + 32)
                for m in range(MT):
                    V.tensor_tensor(gb[:, m], ps[m][:, :], brow[:, 0], ALU.add)
                dve.drain()
                V.tensor_scalar(gb, gb, LIMIT, None, ALU.min)
                dve.drain()
                dve.sem_inc(gate_taken, 1)

            def take_up(e):
                dve.wait_ge(up_done, e + 1)
                for m in range(MT):
                    V.tensor_tensor(hb[:, m], ps[2 + m][:, :], brow[:, 1], ALU.add)
                dve.drain()
                dve.sem_inc(up_taken, 2)
                V.tensor_scalar(hb, hb, LIMIT, -LIMIT, ALU.min, ALU.max)
                dve.drain()
                V.scalar_tensor_tensor(out=hb, in0=hb, scalar=1.0, in1=gb, op0=ALU.add, op1=ALU.mult)
                dve.drain()
                dve.wait_ge(sig_ready, e + 1)
                for m in range(MT):
                    wcol = wt[:, m, ds(e, 1)] if not isinstance(e, int) else wt[:, m, e:e + 1]
                    V.scalar_tensor_tensor(out=hb[:, m], in0=hb[:, m], scalar=wcol, in1=sg[:, m],
                                           op0=ALU.mult, op1=ALU.mult)
                dve.drain()
                dve.sem_inc(hb_ready, 1)

            def add_down(e):
                for n in range(8):
                    av = acc[:, n // 4, (n % 4) * 512:(n % 4) * 512 + 512]
                    dve.wait_ge(dn_ready[n % 2], 4 * e + n // 2 + 1)
                    V.tensor_tensor(av, av, ps[6 + n % 2][:, :], ALU.add).then_inc(dn_taken[n % 2], 1)

            def column(v, m, e):
                return v[:, m, e:e + 1] if isinstance(e, int) else v[:, m, ds(e, 1)]

            def select(e):
                for m in range(MT):
                    V.tensor_scalar(Psel[:, m], slots1, column(pos, m, e), column(sel, m, e), ALU.is_equal, ALU.mult)
                dve.drain()
                dve.sem_inc(p_built, 1)

            def stake_gate(e):
                dve.wait_ge(gate_done, e + 1)
                dve.wait_ge(brow_loaded, 32 * e + 32)
                V.tensor_tensor(sgb[0:CAP], ps[2][0:CAP, :], brow[0:CAP, 0], ALU.add)
                dve.drain()
                V.tensor_scalar(sgb[0:CAP], sgb[0:CAP], LIMIT, None, ALU.min)
                dve.drain()
                dve.sem_inc(gate_taken, 1)

            def stake_up(e):
                dve.wait_ge(up_done, e + 1)
                V.tensor_tensor(shb[0:CAP], ps[3][0:CAP, :], brow[0:CAP, 1], ALU.add)
                for m in range(MT):
                    V.tensor_scalar(Pw[:, m], slots1, column(pos, m, e), column(wt, m, e), ALU.is_equal, ALU.mult)
                dve.drain()
                dve.sem_inc(up_taken, 2)
                V.tensor_scalar(shb[0:CAP], shb[0:CAP], LIMIT, -LIMIT, ALU.min, ALU.max)
                dve.drain()
                V.scalar_tensor_tensor(out=shb[0:CAP], in0=shb[0:CAP], scalar=1.0, in1=sgb[0:CAP],
                                       op0=ALU.add, op1=ALU.mult)
                dve.drain()
                dve.wait_ge(sig_ready, e + 1)
                V.tensor_tensor(shb[0:CAP], shb[0:CAP], ssg[0:CAP], ALU.mult)
                dve.drain()
                dve.sem_inc(hb_ready, 1)

            def add_scatter(e, lo=0, hi=8):
                for n in range(lo, hi):
                    av = acc[:, n // 4, (n % 4) * 512:(n % 4) * 512 + 512]
                    dve.wait_ge(sc_done, 8 * e + n + 1)
                    V.tensor_tensor(av, av, ps[(0, 1, 6, 7)[n % 4]][:, :], ALU.add).then_inc(sc_taken, 1)

            over = dve.value_load(flag[0:1, 0:1], min_val=0, max_val=1)
            with dve.If(over < 1):
                dve.sem_inc(sc_taken, 4)
                select(0)
                stake_gate(0)
                select(1)
                stake_up(0)
                with dve.Fori(1, N_E - 1) as e:
                    stake_gate(e)
                    select(e + 1)
                    add_scatter(e - 1, 0, 6)
                    stake_up(e)
                    add_scatter(e - 1, 6, 8)
                stake_gate(N_E - 1)
                add_scatter(N_E - 2, 0, 6)
                stake_up(N_E - 1)
                add_scatter(N_E - 2, 6, 8)
                add_scatter(N_E - 1)
            with dve.If(over > 0):
                take_gate(0)
                take_up(0)
                with dve.Fori(1, N_E) as e:
                    take_gate(e)
                    add_down(e - 1)
                    take_up(e)
                add_down(N_E - 1)
            dve.wait_ge(ln2_loaded, 32)
            dve.drain()
            for m in range(MT):
                V.scalar_tensor_tensor(out=h1[:, m], in0=h1[:, m], scalar=ALPHA, in1=acc[:, m], op0=ALU.mult, op1=ALU.add)
                dve.drain()
                norm(m, ln2row, MT + m)
                dve.sem_inc(out_ready, 1)


_INS = ['x', 'w_in', 'dn_conv_w', 'dn_a_log', 'dn_dt_bias', 'dn_norm_w', 'w_dn_out', 's5_lam_re', 's5_lam_im',
        's5_log_dt', 's5_b_re', 's5_b_im', 's5_c_re', 's5_c_im', 's5_d', 'w_glu_a', 'w_glu_b', 'w_mix_out',
        'ln1_g', 'ln1_b', 'w_router', 'b_router', 'w_gate', 'b_gate', 'w_up', 'b_up', 'w_down', 'b_down',
        'ln2_g', 'ln2_b']


def kernel(**inputs):
    import numpy as _np
    import concourse.bacc as _bacc
    from concourse import mybir as _mybir
    from concourse.bass_utils import run_bass_kernel_spmd as _run

    nc = _bacc.Bacc("TRN2", target_bir_lowering=False, num_devices=1)
    arrays, args = {}, []
    for name in _INS:
        a = _np.ascontiguousarray(inputs[name])
        arrays[f"in_{name}_dram"] = a
        ap = nc.dram_tensor(f"in_{name}_dram", a.shape, _mybir.dt.from_np(a.dtype), kind="ExternalInput").ap()
        args.append(ap if name == 'x' else ap[0])
    o = nc.dram_tensor("out_0_dram", (1, T, D), F32, kind="ExternalOutput").ap()
    build(nc, *args, o)
    r = _run(nc, [arrays], core_ids=[0])
    return r.results[0]["out_0_dram"]
```
